# Optimizing a Trainium2 kernel written in Bass

```python
import jax, jax.numpy as jnp
from jax import lax
import numpy as np

D_MODEL = 2048
BATCH = 1
SEQ = 256
DEPTH = 2

CHUNK = 64
N_MIXERS = 2
N_LAYERS_A = (DEPTH + 1) // 2
N_LAYERS_B = DEPTH // 2
CONV_A_WIDTH = 31
CONV_B_WIDTH = 3
D_FF = 4 * D_MODEL
PLE_DIM = 256
EPS = 1e-6

kernel_name = "hybrid_conformer_shortconv_trunk"

def rmsnorm(x, g):
    xf = x.astype(jnp.float32)
    r = lax.rsqrt(jnp.mean(xf * xf, axis=-1, keepdims=True) + EPS)
    return (xf * r).astype(x.dtype) * g

def causal_depthwise_conv(x, w):
    k_width, channels = w.shape
    return lax.conv_general_dilated(
        x, w[:, None, :],
        window_strides=(1,),
        padding=[(k_width - 1, 0)],
        dimension_numbers=("NWC", "WIO", "NWC"),
        feature_group_count=channels)

def conformer_conv_module(u, w_pw1, b_pw1, w_dw, b_dw, g_norm, w_pw2, b_pw2):
    a = jnp.einsum("bsd,de->bse", u, w_pw1) + b_pw1
    val, gate = jnp.split(a, 2, axis=-1)
    v = val * jax.nn.sigmoid(gate)
    v = causal_depthwise_conv(v, w_dw) + b_dw
    v = rmsnorm(v, g_norm)
    v = jax.nn.silu(v)
    return jnp.einsum("bsd,de->bse", v, w_pw2) + b_pw2

def short_gated_conv(u, w_in, w_conv, w_out):
    bcv = jnp.einsum("bsd,de->bse", u, w_in)
    gate_b, gate_c, v = jnp.split(bcv, 3, axis=-1)
    y = gate_b * causal_depthwise_conv(gate_c * v, w_conv)
    return jnp.einsum("bsd,de->bse", y, w_out)

def squared_relu_mlp(u, w1, w2):
    hdn = jnp.square(jax.nn.relu(jnp.einsum("bsd,df->bsf", u, w1)))
    return jnp.einsum("bsf,fd->bsd", hdn, w2)

def per_layer_embedding(h, p_i, g_norm, w_proj, w_gate):
    e = jnp.einsum("bsk,kd->bsd", p_i, w_proj)
    g = jax.nn.sigmoid(jnp.einsum("bsd,de->bse", rmsnorm(h, g_norm), w_gate))
    return g * e

def setup_inputs(seed: int = 0) -> dict:
    key = jax.random.key(seed)
    ks = jax.random.split(key, 24)

    def nrm(k, shape, scale):
        return jax.random.normal(k, shape, jnp.float32) * scale

    def gain(k, shape):
        return 1.0 + 0.05 * jax.random.normal(k, shape, jnp.float32)

    D = D_MODEL
    return {
        "x": nrm(ks[0], (BATCH, SEQ, D), 1.0),
        "p": nrm(ks[1], (DEPTH, BATCH, SEQ, PLE_DIM), 1.0),
        "norm_mix": gain(ks[2], (DEPTH, D)),
        "norm_mlp": gain(ks[3], (DEPTH, D)),
        "norm_ple": gain(ks[4], (DEPTH, D)),
        "cf_w_pw1": nrm(ks[5], (N_LAYERS_A, D, 2 * D), D ** -0.5),
        "cf_b_pw1": nrm(ks[6], (N_LAYERS_A, 2 * D), 0.02),
        "cf_w_dw": nrm(ks[7], (N_LAYERS_A, CONV_A_WIDTH, D), CONV_A_WIDTH ** -0.5),
        "cf_b_dw": nrm(ks[8], (N_LAYERS_A, D), 0.02),
        "cf_norm": gain(ks[9], (N_LAYERS_A, D)),
        "cf_w_pw2": nrm(ks[10], (N_LAYERS_A, D, D), D ** -0.5),
        "cf_b_pw2": nrm(ks[11], (N_LAYERS_A, D), 0.02),
        "sc_w_in": nrm(ks[12], (N_LAYERS_B, D, 3 * D), D ** -0.5),
        "sc_w_conv": nrm(ks[13], (N_LAYERS_B, CONV_B_WIDTH, D), CONV_B_WIDTH ** -0.5),
        "sc_w_out": nrm(ks[14], (N_LAYERS_B, D, D), D ** -0.5),
        "mlp_w1": nrm(ks[15], (DEPTH, D, D_FF), D ** -0.5),
        "mlp_w2": nrm(ks[16], (DEPTH, D_FF, D), D_FF ** -0.5),
        "ple_w_proj": nrm(ks[17], (DEPTH, PLE_DIM, D), PLE_DIM ** -0.5),
        "ple_w_gate": nrm(ks[18], (DEPTH, D, D), D ** -0.5),
        "norm_final": gain(ks[19], (D,)),
    }

def reference(x, p, norm_mix, norm_mlp, norm_ple,
              cf_w_pw1, cf_b_pw1, cf_w_dw, cf_b_dw, cf_norm, cf_w_pw2, cf_b_pw2,
              sc_w_in, sc_w_conv, sc_w_out,
              mlp_w1, mlp_w2, ple_w_proj, ple_w_gate, norm_final):
    h = x
    for i in range(DEPTH):
        j = i // N_MIXERS
        u = rmsnorm(h, norm_mix[i])
        if i % N_MIXERS == 0:
            m = conformer_conv_module(u, cf_w_pw1[j], cf_b_pw1[j], cf_w_dw[j], cf_b_dw[j],
                                      cf_norm[j], cf_w_pw2[j], cf_b_pw2[j])
        else:
            m = short_gated_conv(u, sc_w_in[j], sc_w_conv[j], sc_w_out[j])
        h = h + m
        h = h + squared_relu_mlp(rmsnorm(h, norm_mlp[i]), mlp_w1[i], mlp_w2[i])
        h = h + per_layer_embedding(h, p[i], norm_ple[i], ple_w_proj[i], ple_w_gate[i])
    return rmsnorm(h, norm_final)


_drawn_inputs = setup_inputs


def setup_inputs(seed=0):
    import zlib

    import numpy as np

    out = dict(_drawn_inputs(seed))
    spreads = {}
    factors = {'norm_ple': 6.696, 'cf_b_pw1': 3.682}
    for name, (base, spread) in spreads.items():
        noise = np.random.default_rng([zlib.crc32(name.encode()), seed]).standard_normal(out[name].shape)
        drawn = base * np.exp(spread * noise) if base else spread * noise
        out[name] = __import__('jax').numpy.asarray(drawn.astype(out[name].dtype))
    for name, factor in factors.items():
        out[name] = (out[name] * factor).astype(out[name].dtype)
    return out
```

```python
from contextlib import ExitStack

import concourse.bass as bass
from concourse import mybir

F32 = mybir.dt.float32
F32R = mybir.dt.float32r
ALU = mybir.AluOpType
ACT = mybir.ActivationFunctionType
AX = mybir.AxisListType

P = 128
EPS = 1e-6
NB = 512
KC = 16
HALVES = 8
TILES = 4
BLOCKS = 4
SLOTS = 4


FIELDS = ("b", "a", "T", "t", "xh", "s", "sg")


class Place:

    def __init__(self, n):
        self.b, self.a, self.T, self.t, self.xh, self.s, self.sg = (n[f] for f in FIELDS)

    def counts(self):
        return dict(zip(FIELDS, (self.b, self.a, self.T, self.t, self.xh, self.s, self.sg)))


class Unit(Place):

    def __init__(self, kind, at, per):
        super().__init__(at)
        self.kind, self.per = kind, dict(per)

    def shifted(self, by, rounds):
        n = self.counts()
        return Unit(self.kind, {f: n[f] + rounds * by[f] if by[f] else n[f] for f in FIELDS}, self.per)


class Result(Place):

    def __init__(self, unit, j):
        n, per = unit.counts(), unit.per
        super().__init__({f: n[f] + per[f] * j if f in per else n[f] for f in FIELDS})
        self.kind, self.j, self.pair = unit.kind, j, j % 2
        self.transposed = "T" in per


class Steps:

    def __init__(self, engine, sem):
        self.engine, self.sem, self.n, self.emitted = engine, sem, 0, 0

    def mark(self, instruction):
        instruction.then_inc(self.sem, 1)
        self.n = self.n + 1
        self.emitted += 1
        return self.n

    def wait(self, n=None):
        self.engine.wait_ge(self.sem, self.n if n is None else n)

    def loop(self, i, start, per):
        self.kept = (self.n, self.emitted, start, per)
        if per:
            self.n = self.n + (i - start) * per

    def end(self, stop):
        n, emitted, start, per = self.kept
        assert self.emitted - emitted == per, (self.emitted - emitted, per)
        self.n = n + (stop - start) * per


def trunk(nc, t_in, out):
    x, p = t_in["x"], t_in["p"]
    _, SEQ, D = x.shape
    DEPTH, _, _, PLE = p.shape
    WA = t_in["cf_w_dw"].shape[1]
    WB = t_in["sc_w_conv"].shape[1]
    assert SEQ == 2 * P and D == KC * P == BLOCKS * NB and DEPTH == 2 and PLE == 2 * P
    GROUPS = t_in["mlp_w1"].shape[2] // D
    PAD = WA - 1

    ROW_DW, ROW_BDW, ROW_CFN = 0, WA, WA + 1
    ROW_MIX, ROW_MLP, ROW_PLE, ROW_SC = WA + 2, WA + 4, WA + 6, WA + 8
    NROWS = ROW_SC + WB

    at = dict(b=0, a=0, T=BLOCKS, t=0, xh=BLOCKS, s=BLOCKS, sg=0)

    def place(kind, per, blocks=BLOCKS):
        u = Unit(kind, at, dict(per, b=1, a=1))
        for f in FIELDS:
            n = u.per.get(f, 0)
            at[f] += n * BLOCKS if f not in "ba" else blocks
        return u

    pw1 = Unit("glu", dict(at, b=1, a=1), dict(b=2, a=2, T=1, t=1, sg=1))
    EMB_B, EMB_T = 2 * BLOCKS, 2 * BLOCKS - 1
    LAST_GLU_T = EMB_T + 1
    at.update(b=EMB_B + 1, a=EMB_B + HALVES, T=LAST_GLU_T + 1, t=BLOCKS,
              xh=2 * BLOCKS + 1, sg=2 * BLOCKS)
    RES = dict(T=1, t=1, xh=1, s=1)
    pw2 = place("pw2", RES)
    HID = dict(T=1, t=1, xh=1)

    def place_mlp():
        up, down = [], []
        up.append(place("hidden", HID))
        for g in range(GROUPS):
            down_after = g < GROUPS - 1
            down.append(place("add" if down_after else "mlp_out", {} if down_after else RES))
            if down_after:
                up.append(place("hidden", HID))
        return up, down

    mlp = [place_mlp()]
    gate = [place("gate", dict(RES, sg=1))]
    win = Unit("win", at, dict(b=3, a=3, T=2, t=2, xh=1))
    for f, n in dict(b=3, a=3, T=2, t=2, xh=1).items():
        at[f] += n * BLOCKS
    wout = place("w_out", RES)
    mlp.append(place_mlp())
    gate.append(place("gate_last", dict(t=1, s=1, sg=1)))

    NORM_CONV, NORM_MLP, NORM_PLE, NORM_WIN, NORM_FINAL = 1, (2, 5), (3, 6), 4, 7

    def distance(u, v):
        return {f: v.counts()[f] - u.counts()[f] for f in FIELDS}

    ctx = ExitStack()
    with ctx:
        def sb(name, shape, dt=F32):
            return ctx.enter_context(nc.sbuf_tensor(name, shape, dt))

        def sem(name):
            return ctx.enter_context(nc.semaphore(name))

        h = sb("h", [P, 2, D])
        conv = h[:, :, :].rearrange("p m (c n) -> p (m c) n", n=2 * P)
        X = [(sb("a_hi", [P, KC, 2 * P], F32R), sb("a_lo", [P, KC, 2 * P], F32R)),
             (sb("b_hi", [P, KC, 2 * P], F32R), sb("b_lo", [P, KC, 2 * P], F32R))]
        raw = sb("raw", [P, TILES, 4, NB])
        whi = sb("whi", [P, SLOTS, 2, NB], F32R)
        wlo = sb("wlo", [P, SLOTS, 2, NB], F32R)
        emb = sb("emb", [P, DEPTH, 2, D])
        rows = emb[0:NROWS, 0, 0, :]
        vpad = sb("vpad", [P, 4, PAD + 2 * P])
        res = sb("res", [P, 2, NB])
        work = sb("work", [P, 4, NB])
        zb = work[:, 0:2, :]
        val = work[:, 2:4, :]
        bias2 = work[:, :, :].rearrange("p c n -> p (c n)")
        prows = sb("prows", [P, DEPTH, 2, PLE])
        bias = sb("bias", [P, 2, NB])
        junk = sb("junk", [P, NB])
        vec = sb("vec", [P, KC, NROWS])
        ident = sb("ident", [P, P])
        ones = sb("ones", [P, P])
        ss = sb("ss", [P, 2, BLOCKS])
        rinv = sb("rinv", [P, 2])
        mean = sb("mean", [P, 2])
        root = sb("root", [P, 2])
        rb = sb("rb", [P, 2 * P])
        y3 = zb.rearrange("p m (c n) -> p (m c) n", n=2 * P)
        tmps = [y3, val.rearrange("p m (c n) -> p (m c) n", n=2 * P)]
        rb_parts = res[:, 0, 0:2 * P], res[:, 1, 0:2 * P]
        prod = junk[:, :].rearrange("p (u n) -> p u n", u=2)

        acc = ctx.enter_context(nc.psum_tensor("acc", [P, 6, NB], F32))
        tp = ctx.enter_context(nc.psum_tensor("tp", [P, 4, 2 * P], F32))
        ssb = acc[:, 4, 0:2 * P]

        raw_ready = [sem(f"raw_ready{q}") for q in range(TILES)]
        emb_ready = [sem(f"emb_ready{q}") for q in range(TILES)]
        hi_ready, lo_ready, half_used = sem("hi_ready"), sem("lo_ready"), sem("half_used")
        acc_free = sem("acc_free")
        res_ready = sem("res_ready")
        tp_done, tp_free = sem("tp_done"), sem("tp_free")
        xhi_ready, y_ready = sem("xhi_ready"), sem("y_ready")
        ss_ready, junk_written = sem("ss_ready"), sem("junk_written")
        sig_ready = sem("sig_ready")
        vpad_ready, conv_dve, conv_pool = sem("vpad_ready"), sem("conv_dve"), sem("conv_pool")
        n_ready, y_full, y3_ready = sem("n_ready"), sem("y_full"), sem("y3_ready")
        mean_ready, root_ready = sem("mean_ready"), sem("root_ready")
        sq_ready, sq_used = sem("sq_ready"), sem("sq_used")
        const_ready, rows_ready, p_ready, vec_ready = (
            sem("const_ready"), sem("rows_ready"), sem("p_ready"), sem("vec_ready"))
        x_ready = [sem(f"x_ready{j}") for j in range(BLOCKS)]
        bias_ready, bias2_ready = sem("bias_ready"), sem("bias2_ready")
        reload_ready, final_ready, final_done, out_done = (
            sem("reload_ready"), sem("final_ready"), sem("final_done"), sem("out_done"))
        dve_step, pool_step = sem("dve_step"), sem("pool_step")

        block = ctx.enter_context(nc.Block())

        def cols(j):
            return bass.ds(j * NB, NB)

        def xtok(j):
            return x[0, :, j * NB:(j + 1) * NB].rearrange("(m q) n -> q m n", q=P)

        @block.sync
        def _(sp):
            def tile(b, q, src):
                if not (isinstance(b, int) and b == 0):
                    sp.wait_ge(lo_ready, HALVES * b - HALVES + 2 * q + 2)
                nc.sync.dma_start(raw[:, q, :, :], src).then_inc(raw_ready[q], 16)

            def load(b, w, col, row=0):
                for q in range(TILES):
                    tile(b, q, w[bass.ds(row + q * 4 * P, 4 * P), bass.ds(col, NB)]
                         .rearrange("(c r) n -> r c n", r=P))

            def load_unit(unit, w, col=0, row=0):
                with sp.Fori(0, BLOCKS) as j:
                    load(unit.b + j, w, j * NB + col, row)

            def load_mlp(layer):
                up, down = mlp[layer]
                w1, w2 = t_in["mlp_w1"][layer], t_in["mlp_w2"][layer]
                by = distance(up[0], up[1])
                with sp.Fori(0, GROUPS) as g:
                    load_unit(up[0].shifted(by, g), w1, col=g * D)
                    load_unit(down[0].shifted(by, g), w2, row=g * D)

            for j in range(BLOCKS):
                nc.sync.dma_start(h[:, :, j * NB:(j + 1) * NB], xtok(j)).then_inc(x_ready[j], 16)
                if j == 0:
                    w = t_in["cf_w_pw1"][0]
                    load(0, w, 0)
            load(1, w, D)
            with sp.Fori(1, BLOCKS) as j:
                load(2 * j, w, j * NB)
                load(2 * j + 1, w, j * NB + D)
            for q in range(TILES):
                w, n0 = t_in["ple_w_proj"][q // 2], (q % 2) * 2 * NB
                sp.wait_ge(lo_ready, HALVES * EMB_B - HALVES + 2 * q + 2)
                for s, ready in enumerate((raw_ready[q], emb_ready[q])):
                    nc.sync.dma_start(raw[:, q, 2 * s:2 * s + 2, :], w[:, n0 + s * NB:n0 + (s + 1) * NB]
                                      .rearrange("(c r) n -> r c n", r=P)).then_inc(ready, 16)
            load_unit(pw2, t_in["cf_w_pw2"][0])
            load_mlp(0)
            load_unit(gate[0], t_in["ple_w_gate"][0])
            with sp.Fori(1, BLOCKS + 1) as j:
                for part, first in ((0, D), (1, 2 * D), (2, 0)):
                    load(win.b - 3 + 3 * j + part, t_in["sc_w_in"][0], j * NB + first - NB)
            load_unit(wout, t_in["sc_w_out"][0])
            load_mlp(1)
            load_unit(gate[1], t_in["ple_w_gate"][1])
            sp.wait_ge(lo_ready, HALVES * at["b"])
            nc.sync.dma_start(raw[:, 2, :, :].rearrange("p c n -> p (c n)"),
                              t_in["norm_final"].partition_broadcast(P)).then_inc(final_ready, 16)
            for m in range(2):
                sp.wait_ge(final_done, m + 1)
                nc.sync.dma_start(out[0, m * P:(m + 1) * P, :],
                                  raw[:, m, :, :].rearrange("p c n -> p (c n)")).then_inc(out_done, 16)
            sp.wait_ge(out_done, 32)

        @block.tensor
        def _(pe):
            def transpose_group(parts):
                for c, m, src in parts:
                    last = nc.tensor.transpose(tp[:, c, m * P:(m + 1) * P], src, ident[:, :])
                last.then_inc(tp_done, 1)

            def half(b, e, pair, xhi, xlo, chunks, first, last):
                pe.wait_ge(lo_ready, HALVES * b + e + 1)
                for m in range(2):
                    o = acc[:, bass.ds(2 * pair + m, 1), :]
                    s = slice(m * P, (m + 1) * P)
                    for c, k in enumerate(chunks):
                        hi, lo = whi[:, e % SLOTS, c, :], wlo[:, e % SLOTS, c, :]
                        nc.tensor.matmul(o, xhi[:, k, s], hi, start=first and c == 0, stop=False)
                        nc.tensor.matmul(o, xhi[:, k, s], lo, start=False, stop=False)
                        mm = nc.tensor.matmul(o, xlo[:, k, s], hi, start=False, stop=last and c == 1)
                mm.then_inc(half_used, 1)

            def multiply(b, a, pair, xin, pre=None, ready=None):
                xhi, xlo = xin
                if not (isinstance(a, int) and a < 2):
                    pe.wait_ge(acc_free, a - 1)
                for e in range(HALVES):
                    if ready and e % 2 == 0:
                        pe.wait_ge(ready[0], ready[1] + e // 2 + 1)
                    half(b, e, pair, xhi, xlo, (2 * e, 2 * e + 1), e == 0, e == HALVES - 1)
                    if e == 3 and pre is not None:
                        pe.wait_ge(res_ready, pre[1] + 1)
                        pe.wait_ge(tp_free, pre[0])
                        transpose_group((c, m, res[:, m, c * P:(c + 1) * P])
                                        for c in range(4) for m in range(2))

            def multiply_unit(unit, xin, ready, before=None):
                pre = (before.T, before.t) if before is not None and before.transposed else None
                multiply(unit.b, unit.a, 0, xin, pre, ready)
                with pe.Fori(1, BLOCKS) as j:
                    r = Result(unit, j - 1)
                    multiply(unit.b + j, unit.a + j, j % 2, xin,
                             (r.T, r.t) if r.transposed else None)

            def multiply_mlp(layer, u, ready, before):
                up, down = mlp[layer]
                hid = 1 - u
                by = distance(up[0], up[1])
                multiply_unit(up[0], X[u], ready, before)
                with pe.Fori(0, GROUPS - 1) as g:
                    w2, w1 = down[0].shifted(by, g), up[1].shifted(by, g)
                    multiply_unit(w2, X[hid], (tp_free, up[0].shifted(by, g).T),
                                  Result(up[0].shifted(by, g), BLOCKS - 1))
                    multiply_unit(w1, X[u], None, Result(w2, BLOCKS - 1))
                multiply_unit(down[-1], X[hid], (tp_free, up[-1].T), Result(up[-1], BLOCKS - 1))

            pe.wait_ge(const_ready, 4)
            pe.wait_ge(rows_ready, 16 * 7)
            for c in range(KC):
                v = tp[:, 2 * (c // 8):2 * (c // 8) + 2, :].rearrange("p c n -> p (c n)")
                last = nc.tensor.transpose(v[:, (c % 8) * NROWS:(c % 8 + 1) * NROWS],
                                           rows[:, c * P:(c + 1) * P], ident[0:NROWS, 0:NROWS])
            last.then_inc(vec_ready, 1)
            for j in range(BLOCKS):
                pe.wait_ge(x_ready[j], 16)
                if j == 0:
                    pe.wait_ge(vec_ready, 2)
                else:
                    pe.wait_ge(tp_free, j)
                transpose_group((c, m, h[:, m, (4 * j + c) * P:(4 * j + c + 1) * P])
                                for c in range(4) for m in range(2))

            multiply(0, 0, 0, X[0], None, (tp_free, 0))
            multiply(1, 1, 1, X[0])
            with pe.Fori(1, BLOCKS) as j:
                r = Result(pw1, j - 1)
                multiply(2 * j, 2 * j, 0, X[0], (r.T, r.t))
                multiply(2 * j + 1, 2 * j + 1, 1, X[0])

            pe.wait_ge(p_ready, 16 * DEPTH)
            pe.wait_ge(tp_free, EMB_T)
            transpose_group((2 * l + c, m, prows[:, l, m, c * P:(c + 1) * P])
                            for l in range(DEPTH) for c in range(2) for m in range(2))
            pe.wait_ge(tp_free, EMB_T + 1)
            for e in range(HALVES):
                pe.wait_ge(acc_free, EMB_B + e - 1)
                l = e // BLOCKS
                half(EMB_B, e, e % 2, X[0][0], X[0][1], (2 * l, 2 * l + 1), True, True)
                if e == 1:
                    pe.wait_ge(res_ready, BLOCKS)
                    transpose_group((c, m, res[:, m, c * P:(c + 1) * P])
                                    for c in range(4) for m in range(2))
            for j in range(BLOCKS):
                pe.wait_ge(sq_ready, j + 1)
                for c in range(4):
                    mm = nc.tensor.matmul(ssb, ones[:, :], tmps[j % 2][:, c, :],
                                          start=j == 0 and c == 0, stop=j == BLOCKS - 1 and c == 3)
                mm.then_inc(sq_used, 1)

            multiply_unit(pw2, X[1], (y_ready, 0))
            multiply_mlp(0, 0, (tp_free, pw2.T), Result(pw2, BLOCKS - 1))
            multiply_unit(gate[0], X[0], (tp_free, mlp[0][1][-1].T), Result(mlp[0][1][-1], BLOCKS - 1))

            r = Result(gate[0], BLOCKS - 1)
            multiply(win.b, win.a, 0, X[1], (r.T, r.t), (tp_free, gate[0].T))
            multiply(win.b + 1, win.a + 1, 1, X[1])
            multiply(win.b + 2, win.a + 2, 2, X[1], (win.T, win.t))
            with pe.Fori(1, BLOCKS) as j:
                multiply(win.b + 3 * j, win.a + 3 * j, 0, X[1], (win.T + 2 * j - 1, win.t + 2 * j - 1))
                multiply(win.b + 3 * j + 1, win.a + 3 * j + 1, 1, X[1])
                multiply(win.b + 3 * j + 2, win.a + 3 * j + 2, 2, X[1], (win.T + 2 * j, win.t + 2 * j))
            multiply(wout.b, wout.a, 0, X[0], (wout.T - 1, wout.t - 1), (y_ready, BLOCKS))
            with pe.Fori(1, BLOCKS) as j:
                r = Result(wout, j - 1)
                multiply(wout.b + j, wout.a + j, j % 2, X[0], (r.T, r.t))
            multiply_mlp(1, 1, (tp_free, wout.T), Result(wout, BLOCKS - 1))
            multiply_unit(gate[1], X[1], (tp_free, mlp[1][1][-1].T), Result(mlp[1][1][-1], BLOCKS - 1))

        @block.scalar
        def _(act):
            def split_hi(b, e):
                if e % 2 == 0:
                    act.wait_ge(raw_ready[e // 2], 16 * b + 16)
                elif isinstance(b, int) and b == EMB_B:
                    act.wait_ge(emb_ready[e // 2], 16)
                if not (isinstance(b, int) and b == 0 and e < SLOTS):
                    act.wait_ge(half_used, HALVES * b + e + 1 - SLOTS)
                nc.scalar.activation(whi[:, e % SLOTS, :, :],
                                     raw[:, e // 2, 2 * (e % 2):2 * (e % 2) + 2, :],
                                     ACT.Copy).then_inc(hi_ready, 1)

            def squares(n, src, j):
                for m in range(2):
                    if m:
                        act.wait_ge(junk_written, n + 1)
                    elif not (isinstance(n, int) and n == 0):
                        act.wait_ge(ss_ready, n)
                    ins = nc.scalar.activation(junk[:, :], src(m), ACT.Square,
                                               accum_out=ss[:, m, bass.ds(j, 1)])
                    ins.then_inc(ss_ready if m else junk_written, 1)

            def process(r):
                if r.kind == "hidden":
                    act.wait_ge(acc_free, r.a + 1)
                    act.wait_ge(tp_done, r.T)
                    nc.scalar.activation(res[:, :, :], zb, ACT.Square).then_inc(res_ready, 1)
                if r.kind in ("glu", "gate", "gate_last"):
                    act.wait_ge(acc_free, r.a + 1)
                    nc.scalar.activation(zb, zb, ACT.Sigmoid).then_inc(sig_ready, 1)
                if r.kind in ("pw2", "mlp_out", "w_out", "gate", "gate_last"):
                    act.wait_ge(res_ready, r.t + 1)
                    nc.scalar.activation(h[:, :, cols(r.j)], res[:, :, :], ACT.Copy)
                    squares(r.s, lambda m: res[:, m, :], r.j)

            def operand_hi(T, j, dst, gain=None):
                act.wait_ge(tp_done, T + 1)
                if gain is None:
                    last = nc.scalar.activation(dst[0][:, bass.ds(4 * j, 4), :], tp[:, :, :], ACT.Copy)
                else:
                    for c in range(4):
                        last = nc.scalar.activation(
                            dst[0][:, bass.ds(4 * j + c, 1), :], tp[:, c:c + 1, :], ACT.Copy,
                            scale=vec[:, bass.ds(4 * j + c, 1), gain])
                last.then_inc(xhi_ready, 1)

            def to_vpad(T, n, pool_groups):
                act.wait_ge(tp_done, T + 1)
                act.wait_ge(conv_dve, n + 1)
                act.wait_ge(conv_pool, pool_groups + 1)
                nc.scalar.activation(vpad[:, :, PAD:], tp[:, :, :], ACT.Copy).then_inc(vpad_ready, 1)
                act.wait_ge(vpad_ready, n + 1)
                nc.scalar.sem_inc(tp_free, 1)

            def run(b, before=None, after=None):
                for e in range(HALVES):
                    if e == 3 and before:
                        before()
                    if e == 7 and after:
                        after()
                    split_hi(b, e)

            def take_root(n, src=None, dst=None):
                act.wait_ge(mean_ready, n + 1)
                nc.scalar.activation(root[:, :] if dst is None else dst, mean[:, :] if src is None else src,
                                     ACT.Sqrt).then_inc(root_ready, 1)

            def run_behind(b, r, dst, gain=None, new_norm=None):
                def after():
                    if r.transposed:
                        operand_hi(r.T, r.j, dst, gain)
                    if new_norm is not None:
                        take_root(new_norm)
                run(b, lambda: process(r), after)

            def run_unit(u, dst, gain, prev, prev_dst, prev_gain, new_norm=None):
                run_behind(u.b, Result(prev, BLOCKS - 1), prev_dst, prev_gain, new_norm)
                with act.Fori(1, BLOCKS) as j:
                    run_behind(u.b + j, Result(u, j - 1), dst, gain)

            def run_mlp(layer, u, prev):
                up, down = mlp[layer]
                hid, gain = X[1 - u], ROW_PLE + layer
                by = distance(up[0], up[1])
                run_unit(up[0], hid, None, prev, X[u], ROW_MLP + layer, NORM_MLP[layer])
                with act.Fori(0, GROUPS - 1) as g:
                    w2, w1 = down[0].shifted(by, g), up[1].shifted(by, g)
                    run_unit(w2, None, None, up[0].shifted(by, g), hid, None)
                    run_unit(w1, hid, None, w2, None, None)
                run_unit(down[-1], X[u], gain, up[-1], hid, None)

            for r0, src in [(ROW_DW, t_in["cf_w_dw"][0]), (ROW_BDW, t_in["cf_b_dw"]),
                            (ROW_CFN, t_in["cf_norm"]), (ROW_MIX, t_in["norm_mix"]),
                            (ROW_MLP, t_in["norm_mlp"]), (ROW_PLE, t_in["norm_ple"]),
                            (ROW_SC, t_in["sc_w_conv"][0])]:
                nc.scalar.dma_start(rows[r0:r0 + src.shape[0], :], src).then_inc(rows_ready, 16)
            for l in range(DEPTH):
                nc.scalar.dma_start(prows[:, l, :, :],
                                    p[l, 0].rearrange("(m q) n -> q m n", q=P)).then_inc(p_ready, 16)
            for j in range(BLOCKS):
                act.wait_ge(x_ready[j], 16)
                squares(j, lambda m: h[:, m, j * NB:(j + 1) * NB], j)
                if j == 0:
                    act.wait_ge(vec_ready, 2)
                operand_hi(j, j, X[0], ROW_MIX)
            take_root(0)

            run(0)
            run(1)
            with act.Fori(1, BLOCKS) as j:
                r = Result(pw1, j - 1)
                run(2 * j, lambda: process(r), lambda: to_vpad(r.T, r.j, r.j))
                run(2 * j + 1)

            def embedding_out(e):
                act.wait_ge(acc_free, EMB_B + e)
                act.wait_ge(half_used, HALVES * EMB_B + e + 1)
                nc.scalar.activation(emb[:, e // BLOCKS, :, (e % BLOCKS) * NB:(e % BLOCKS + 1) * NB],
                                     acc[:, 2 * (e % 2):2 * (e % 2) + 2, :],
                                     ACT.Copy).then_inc(acc_free, 1)

            for e in range(3):
                split_hi(EMB_B, e)
            process(Result(pw1, BLOCKS - 1))
            operand_hi(EMB_T, 0, X[0])
            split_hi(EMB_B, 3)
            embedding_out(0)
            split_hi(EMB_B, 4)
            embedding_out(1)
            to_vpad(LAST_GLU_T, BLOCKS - 1, BLOCKS - 1)
            for e in range(5, HALVES):
                split_hi(EMB_B, e)
                embedding_out(e - 3)
            for e in range(HALVES - 3, HALVES):
                embedding_out(e)
            for j in range(BLOCKS):
                if j == BLOCKS - 1:
                    for e in range(SLOTS):
                        split_hi(pw2.b, e)
                act.wait_ge(conv_dve, j + 2)
                act.wait_ge(conv_pool, j + 2)
                if j >= 2:
                    act.wait_ge(sq_used, j - 1)
                nc.scalar.activation(tmps[j % 2], conv[:, 4 * j:4 * j + 4, :],
                                     ACT.Square).then_inc(sq_ready, 1)

            def swish_sigmoid(j):
                act.wait_ge(n_ready, j + 1)
                act.wait_ge(sq_used, BLOCKS)
                if j >= 2:
                    act.wait_ge(y_full, j - 1)
                nc.scalar.activation(tmps[j % 2], conv[:, 4 * j:4 * j + 4, :],
                                     ACT.Sigmoid).then_inc(sig_ready, 1)

            def swish_hi(j):
                act.wait_ge(y_full, j + 1)
                nc.scalar.activation(X[1][0][:, 4 * j:4 * j + 4, :], conv[:, 4 * j:4 * j + 4, :],
                                     ACT.Copy).then_inc(xhi_ready, 1)

            take_root(NORM_CONV, *rb_parts)
            swish_sigmoid(0)
            for j in range(1, BLOCKS):
                swish_sigmoid(j)
                swish_hi(j - 1)
            swish_hi(BLOCKS - 1)
            for e in range(SLOTS, HALVES):
                split_hi(pw2.b, e)
            with act.Fori(1, BLOCKS) as j:
                run_behind(pw2.b + j, Result(pw2, j - 1), X[0], ROW_MLP)
            run_mlp(0, 0, pw2)
            run_unit(gate[0], X[1], ROW_MIX + 1, mlp[0][1][-1], X[0], ROW_PLE, NORM_PLE[0])

            def short_out_hi(j):
                act.wait_ge(y3_ready, j + 1)
                nc.scalar.activation(X[0][0][:, bass.ds(4 * j, 4), :], y3, ACT.Copy).then_inc(xhi_ready, 1)

            run_behind(win.b, Result(gate[0], BLOCKS - 1), X[1], ROW_MIX + 1, NORM_WIN)
            run(win.b + 1)
            run(win.b + 2, None, lambda: to_vpad(win.T, BLOCKS, BLOCKS))
            with act.Fori(1, BLOCKS) as j:
                run(win.b + 3 * j, None, lambda: short_out_hi(j - 1))
                run(win.b + 3 * j + 1)
                run(win.b + 3 * j + 2, None, lambda: to_vpad(win.T + 2 * j, j + BLOCKS, BLOCKS))
            run(wout.b, None, lambda: short_out_hi(BLOCKS - 1))
            with act.Fori(1, BLOCKS) as j:
                run_behind(wout.b + j, Result(wout, j - 1), X[1], ROW_MLP + 1)
            run_mlp(1, 1, wout)
            run_unit(gate[1], None, None, mlp[1][1][-1], X[1], ROW_PLE + 1, NORM_PLE[1])
            process(Result(gate[1], BLOCKS - 1))
            take_root(NORM_FINAL)

        @block.vector
        def _(dve):
            steps = Steps(dve, dve_step)

            def split_lo(b, e):
                dve.wait_ge(hi_ready, HALVES * b + e + 1)
                nc.vector.tensor_tensor(wlo[:, e % SLOTS, :, :],
                                        raw[:, e // 2, 2 * (e % 2):2 * (e % 2) + 2, :],
                                        whi[:, e % SLOTS, :, :].bitcast(F32),
                                        ALU.subtract).then_inc(lo_ready, 1)

            def product(b, a):
                dve.wait_ge(half_used, HALVES * b + HALVES)
                if not (isinstance(a, int) and a == 0):
                    dve.wait_ge(acc_free, a)

            def pair_half(pair, m):
                return acc[:, bass.ds(2 * pair + m, 1), :]

            def scaled(dst, pair, bias_row=None):
                for m in range(2):
                    if bias_row is None:
                        last = nc.vector.tensor_scalar(dst[:, m:m + 1, :], pair_half(pair, m),
                                                       rinv[:, m:m + 1], None, ALU.mult)
                    else:
                        last = nc.vector.scalar_tensor_tensor(
                            dst[:, m:m + 1, :], pair_half(pair, m), rinv[:, m:m + 1],
                            bias[:, bias_row:bias_row + 1, :], ALU.mult, ALU.add)
                last.then_inc(acc_free, 1)

            def process(r):
                product(r.b, r.a)
                both = acc[:, bass.ds(2 * r.pair, 2), :]
                here = h[:, :, cols(r.j)]
                if r.kind == "hidden":
                    dve.wait_ge(res_ready, r.t)
                    for m in range(2):
                        last = nc.vector.tensor_scalar(zb[:, m:m + 1, :], pair_half(r.pair, m),
                                                       rinv[:, m:m + 1], 0.0, ALU.mult, ALU.max)
                    last.then_inc(acc_free, 1)
                    return
                if r.kind == "add":
                    dve.wait_ge(ss_ready, r.s)
                    nc.vector.tensor_tensor(here, both, here, ALU.add).then_inc(acc_free, 1)
                    return
                if r.kind in ("gate", "gate_last"):
                    scaled(zb, r.pair)
                    dve.wait_ge(sig_ready, r.sg + 1)
                    steps.mark(nc.vector.tensor_tensor(zb, zb, emb[:, 0 if r.kind == "gate" else 1, :, cols(r.j)],
                                                       ALU.mult))
                    steps.wait()
                dve.wait_ge(tp_done, r.T)
                dve.wait_ge(ss_ready, r.s)
                if r.kind in ("gate", "gate_last"):
                    nc.vector.tensor_tensor(res[:, :, :], zb, here, ALU.add).then_inc(res_ready, 1)
                    return
                nc.vector.tensor_tensor(res[:, :, :], both, here, ALU.add).then_inc(acc_free, 1)
                dve.wait_ge(acc_free, r.a + 1)
                if r.kind == "pw2":
                    nc.vector.tensor_tensor(res[:, :, :], res[:, :, :],
                                            bias2[:, cols(r.j)].unsqueeze(1).to_broadcast([P, 2, NB]),
                                            ALU.add).then_inc(res_ready, 1)
                else:
                    nc.vector.sem_inc(res_ready, 1)

            def operand_lo(xh, j, dst, gain=None):
                dve.wait_ge(xhi_ready, xh + 1)
                if gain is None:
                    last = nc.vector.tensor_tensor(dst[1][:, bass.ds(4 * j, 4), :], tp[:, :, :],
                                                   dst[0][:, bass.ds(4 * j, 4), :].bitcast(F32),
                                                   ALU.subtract)
                else:
                    for c in range(4):
                        last = nc.vector.scalar_tensor_tensor(
                            dst[1][:, bass.ds(4 * j + c, 1), :], tp[:, c:c + 1, :],
                            vec[:, bass.ds(4 * j + c, 1), gain],
                            dst[0][:, bass.ds(4 * j + c, 1), :].bitcast(F32), ALU.mult, ALU.subtract)
                last.then_inc(tp_free, 1)

            def inverse_root(n, total, m, y, t):
                nc.vector.tensor_scalar(m, total, 1.0 / D, EPS, ALU.mult, ALU.add).then_inc(mean_ready, 1)
                dve.wait_ge(root_ready, n + 1)
                steps.mark(nc.vector.reciprocal(y, t))
                steps.wait()
                steps.mark(nc.vector.tensor_tensor(t, y, y, ALU.mult))
                steps.wait()
                steps.mark(nc.vector.tensor_tensor(t, t, m, ALU.mult))
                steps.wait()
                steps.mark(nc.vector.tensor_scalar(t, t, -0.5, 1.5, ALU.mult, ALU.add))
                steps.wait()
                steps.mark(nc.vector.tensor_tensor(y, y, t, ALU.mult))
                steps.wait()

            def norm(n, groups):
                dve.wait_ge(ss_ready, groups)
                steps.mark(nc.vector.tensor_reduce(rinv[:, :], ss[:, :, :], AX.X, ALU.add))
                steps.wait()
                inverse_root(n, rinv[:, :], mean[:, :], rinv[:, :], root[:, :])

            def run(b, before=None, after=None, between=None):
                for e in range(HALVES):
                    if e == 3 and before:
                        before()
                    if e == 7 and after:
                        after()
                    split_lo(b, e)
                    if between:
                        between(e)

            def run_behind(b, r, dst, gain=None, new_norm=None):
                def after():
                    if r.transposed:
                        operand_lo(r.xh, r.j, dst, gain)
                    if new_norm is not None:
                        norm(*new_norm)
                run(b, lambda: process(r), after)

            def run_unit(u, dst, gain, prev, prev_dst, prev_gain, new_norm=None):
                run_behind(u.b, Result(prev, BLOCKS - 1), prev_dst, prev_gain,
                           None if new_norm is None else (new_norm, u.s))
                with dve.Fori(1, BLOCKS) as j:
                    steps.loop(j, 1, 1 if u.kind in ("gate", "gate_last") else 0)
                    run_behind(u.b + j, Result(u, j - 1), dst, gain)
                steps.end(BLOCKS)

            def run_mlp(layer, u, prev):
                up, down = mlp[layer]
                hid, gain = X[1 - u], ROW_PLE + layer
                by = distance(up[0], up[1])
                run_unit(up[0], hid, None, prev, X[u], ROW_MLP + layer, NORM_MLP[layer])
                with dve.Fori(0, GROUPS - 1) as g:
                    w2, w1 = down[0].shifted(by, g), up[1].shifted(by, g)
                    run_unit(w2, None, None, up[0].shifted(by, g), hid, None)
                    run_unit(w1, hid, None, w2, None, None)
                run_unit(down[-1], X[u], gain, up[-1], hid, None)

            nc.vector.sem_inc(conv_dve, 1)
            dve.wait_ge(vec_ready, 1)
            for bank in range(2):
                v = tp[:, 2 * bank:2 * bank + 2, :].rearrange("p c n -> p (c n)")
                last = nc.vector.tensor_copy(vec[:, 8 * bank:8 * bank + 8, :].rearrange("p c r -> p (c r)"),
                                             v[:, 0:8 * NROWS])
            last.then_inc(vec_ready, 1)
            for j in range(BLOCKS):
                operand_lo(j, j, X[0], ROW_MIX)
            norm(0, BLOCKS)

            def value(j):
                product(2 * j, 2 * j)
                dve.wait_ge(bias_ready, 32 * j + 32)
                scaled(val, 0, 0)

            def glu(r):
                product(r.b, r.a)
                scaled(zb, 1, 1)
                dve.wait_ge(sig_ready, r.sg + 1)
                dve.wait_ge(tp_done, r.T)
                nc.vector.tensor_tensor(res[:, :, :], val, zb, ALU.mult).then_inc(res_ready, 1)

            def taps(j, first, stop):
                for k in range(first, stop):
                    if k:
                        steps.wait()
                    for c in range(3):
                        o = conv[:, bass.ds(4 * j + c, 1), :]
                        w = vec[:, bass.ds(4 * j + c, 1), ROW_DW + k]
                        src = vpad[:, c:c + 1, k:k + 2 * P]
                        if k == 0:
                            ins = nc.vector.tensor_scalar(o, src, w, vec[:, bass.ds(4 * j + c, 1), ROW_BDW],
                                                          ALU.mult, ALU.add)
                        else:
                            ins = nc.vector.scalar_tensor_tensor(o, src, w, o, ALU.mult, ALU.add)
                        if k == WA - 1 and c == 2:
                            ins.then_inc(conv_dve, 1)
                        else:
                            steps.mark(ins)

            cuts = [0, 3] + [3 + (WA - 3) * (e + 1) // HALVES for e in range(HALVES)]

            def first_taps(j):
                dve.wait_ge(vpad_ready, j + 1)
                taps(j, cuts[0], cuts[1])

            run(0)
            run(1, lambda: value(0))
            with dve.Fori(1, BLOCKS) as j:
                steps.loop(j, 1, 3 * WA - 1)
                r = Result(pw1, j - 1)
                run(2 * j, lambda: glu(r), None, lambda e: first_taps(r.j) if e == 7 else None)
                run(2 * j + 1, lambda: value(j), None, lambda e: taps(r.j, cuts[e + 1], cuts[e + 2]))
            steps.end(BLOCKS)

            r = Result(pw1, BLOCKS - 1)
            for e in range(3):
                split_lo(EMB_B, e)
            glu(r)
            operand_lo(BLOCKS, 0, X[0])
            split_lo(EMB_B, 3)
            split_lo(EMB_B, 4)
            dve.wait_ge(vpad_ready, BLOCKS)
            for e in range(5, HALVES):
                taps(BLOCKS - 1, 5 * (e - 5), 5 * (e - 4))
                split_lo(EMB_B, e)
            taps(BLOCKS - 1, 5 * (HALVES - 5), WA)
            for e in range(SLOTS):
                split_lo(pw2.b, e)
            dve.wait_ge(sq_used, BLOCKS)
            inverse_root(NORM_CONV, ssb, rb_parts[0], rb[:, :], rb_parts[1])

            def normalise(j):
                dve.wait_ge(conv_pool, j + 2)
                dve.wait_ge(conv_dve, j + 2)
                for c in range(4 * j, 4 * j + 4):
                    last = nc.vector.scalar_tensor_tensor(conv[:, c, :], conv[:, c, :],
                                                          vec[:, c, ROW_CFN:ROW_CFN + 1], rb[:, :],
                                                          ALU.mult, ALU.mult)
                last.then_inc(n_ready, 1)

            def swish(j):
                dve.wait_ge(sig_ready, BLOCKS + j + 1)
                g = conv[:, 4 * j:4 * j + 4, :]
                nc.vector.tensor_tensor(g, g, tmps[j % 2], ALU.mult).then_inc(y_full, 1)

            def swish_lo(j):
                dve.wait_ge(xhi_ready, BLOCKS + 1 + j + 1)
                dve.wait_ge(y_full, j + 1)
                nc.vector.tensor_tensor(X[1][1][:, 4 * j:4 * j + 4, :], conv[:, 4 * j:4 * j + 4, :],
                                        X[1][0][:, 4 * j:4 * j + 4, :].bitcast(F32),
                                        ALU.subtract).then_inc(y_ready, 1)

            normalise(0)
            for j in range(BLOCKS):
                if j + 1 < BLOCKS:
                    normalise(j + 1)
                swish(j)
                if j:
                    swish_lo(j - 1)
            swish_lo(BLOCKS - 1)
            for e in range(SLOTS, HALVES):
                split_lo(pw2.b, e)
            dve.wait_ge(reload_ready, 32)
            dve.wait_ge(bias2_ready, 16)
            with dve.Fori(1, BLOCKS) as j:
                run_behind(pw2.b + j, Result(pw2, j - 1), X[0], ROW_MLP)
            run_mlp(0, 0, pw2)
            run_unit(gate[0], X[1], ROW_MIX + 1, mlp[0][1][-1], X[0], ROW_PLE, NORM_PLE[0])

            def gate_c(a):
                product(a[0], a[1])
                scaled(val, 0)

            def c_times_v(j):
                product(win.b + 3 * j + 1, win.a + 3 * j + 1)
                dve.wait_ge(tp_done, win.T + 2 * j)
                for m in range(2):
                    last = nc.vector.scalar_tensor_tensor(res[:, m:m + 1, :], pair_half(1, m), rinv[:, m:m + 1],
                                                          val[:, m:m + 1, :], ALU.mult, ALU.mult)
                last.then_inc(acc_free, 1)
                dve.wait_ge(acc_free, win.a + 3 * j + 2)
                nc.vector.sem_inc(res_ready, 1)

            def gate_b(j):
                product(win.b + 3 * j + 2, win.a + 3 * j + 2)
                dve.wait_ge(tp_done, win.T + 2 * j + 1)
                scaled(res, 2)
                dve.wait_ge(acc_free, win.a + 3 * j + 3)
                nc.vector.sem_inc(res_ready, 1)

            def short_taps(j):
                dve.wait_ge(vpad_ready, j + BLOCKS + 1)
                for k in range(WB):
                    if k:
                        steps.wait()
                    for c in range(4):
                        w = vec[:, bass.ds(4 * j + c, 1), ROW_SC + k]
                        src = vpad[:, c:c + 1, PAD - WB + 1 + k:PAD - WB + 1 + k + 2 * P]
                        o = y3[:, c:c + 1, :]
                        if k == 0:
                            ins = nc.vector.tensor_scalar(o, src, w, None, ALU.mult)
                        else:
                            ins = nc.vector.scalar_tensor_tensor(o, src, w, o, ALU.mult, ALU.add)
                        if k == WB - 1 and c == 3:
                            ins.then_inc(conv_dve, 1)
                        else:
                            steps.mark(ins)

            def short_out(j):
                dve.wait_ge(tp_done, win.T + 2 * j + 2)
                dve.wait_ge(conv_dve, j + BLOCKS + 2)
                steps.mark(nc.vector.tensor_tensor(y3, tp[:, :, :], y3, ALU.mult))
                steps.wait()
                nc.vector.sem_inc(tp_free, 1)
                nc.vector.sem_inc(y3_ready, 1)
                dve.wait_ge(xhi_ready, win.xh + j + 1)
                nc.vector.tensor_tensor(X[0][1][:, bass.ds(4 * j, 4), :], y3,
                                        X[0][0][:, bass.ds(4 * j, 4), :].bitcast(F32),
                                        ALU.subtract).then_inc(y_ready, 1)

            run_behind(win.b, Result(gate[0], BLOCKS - 1), X[1], ROW_MIX + 1, (NORM_WIN, win.s))
            run(win.b + 1, lambda: gate_c((win.b, win.a)))
            run(win.b + 2, lambda: c_times_v(0), None, lambda e: short_taps(0) if e == 7 else None)
            with dve.Fori(1, BLOCKS) as j:
                steps.loop(j, 1, 4 * WB)
                run(win.b + 3 * j, lambda: gate_b(j - 1), lambda: short_out(j - 1))
                run(win.b + 3 * j + 1, lambda: gate_c((win.b + 3 * j, win.a + 3 * j)))
                run(win.b + 3 * j + 2, lambda: c_times_v(j), None,
                    lambda e: short_taps(j) if e == 7 else None)
            steps.end(BLOCKS)
            run(wout.b, lambda: gate_b(BLOCKS - 1), lambda: short_out(BLOCKS - 1))
            with dve.Fori(1, BLOCKS) as j:
                run_behind(wout.b + j, Result(wout, j - 1), X[1], ROW_MLP + 1)
            run_mlp(1, 1, wout)
            run_unit(gate[1], None, None, mlp[1][1][-1], X[1], ROW_PLE + 1, NORM_PLE[1])
            process(Result(gate[1], BLOCKS - 1))
            norm(NORM_FINAL, at["s"])
            dve.wait_ge(final_ready, 16)
            flat = raw[:, :, :, :].rearrange("p q c n -> p q (c n)")
            for m in range(2):
                nc.vector.scalar_tensor_tensor(flat[:, m, :], h[:, m, :], rinv[:, m:m + 1], flat[:, 2, :],
                                               ALU.mult, ALU.mult).then_inc(final_done, 1)

        @block.gpsimd
        def _(pool):
            steps = Steps(pool, pool_step)
            nc.gpsimd.sem_inc(conv_pool, 1)
            nc.gpsimd.memset(ident[:, :], 0.0).then_inc(const_ready, 1)
            nc.gpsimd.memset(ones[:, :], 1.0).then_inc(const_ready, 1)
            nc.gpsimd.memset(vpad[:, :, 0:PAD], 0.0).then_inc(const_ready, 1)
            pool.wait_ge(const_ready, 3)
            nc.gpsimd.affine_select(out=ident[:, :], in_=ident[:, :], compare_op=ALU.not_equal, fill=1.0,
                                    base=0, pattern=[[-1, P]], channel_multiplier=1).then_inc(const_ready, 1)

            def load_bias(j):
                for half in range(2):
                    nc.gpsimd.dma_start(bias[:, half, :], t_in["cf_b_pw1"][0, bass.ds(j * NB + half * D, NB)]
                                        .partition_broadcast(P)).then_inc(bias_ready, 16)

            def convolve(j):
                o = conv[:, bass.ds(4 * j + 3, 1), :]

                def per_channel(row):
                    return vec[:, bass.ds(4 * j + 3, 1), row:row + 1].to_broadcast([P, 1, 2 * P])

                pool.wait_ge(vpad_ready, j + 1)
                steps.mark(nc.gpsimd.tensor_tensor(prod[:, 0:1, :], vpad[:, 3:4, 0:2 * P],
                                                   per_channel(ROW_DW), ALU.mult))
                steps.wait()
                steps.mark(nc.gpsimd.tensor_tensor(o, prod[:, 0:1, :], per_channel(ROW_BDW), ALU.add))
                for k in range(1, WA):
                    steps.mark(nc.gpsimd.tensor_tensor(prod[:, k % 2:k % 2 + 1, :], vpad[:, 3:4, k:k + 2 * P],
                                                       per_channel(ROW_DW + k), ALU.mult))
                    steps.wait()
                    last = nc.gpsimd.tensor_tensor(o, prod[:, k % 2:k % 2 + 1, :], o, ALU.add)
                    if k == WA - 1:
                        last.then_inc(conv_pool, 1)
                    else:
                        steps.mark(last)

            load_bias(0)
            pool.wait_ge(const_ready, 4)
            pool.wait_ge(vec_ready, 2)
            for j in range(1, BLOCKS):
                pool.wait_ge(acc_free, 2 * j)
                load_bias(j)
                convolve(j - 1)
            convolve(BLOCKS - 1)
            for m in range(2):
                pool.wait_ge(y_ready, 2 * m + 2)
                nc.gpsimd.dma_start(h[:, m, :], x[0, m * P:(m + 1) * P, :]).then_inc(reload_ready, 16)
            nc.gpsimd.dma_start(bias2, t_in["cf_b_pw2"][0].partition_broadcast(P)).then_inc(bias2_ready, 16)


_INS = ["x", "p", "norm_mix", "norm_mlp", "norm_ple", "cf_w_pw1", "cf_b_pw1", "cf_w_dw", "cf_b_dw",
        "cf_norm", "cf_w_pw2", "cf_b_pw2", "sc_w_in", "sc_w_conv", "sc_w_out", "mlp_w1", "mlp_w2",
        "ple_w_proj", "ple_w_gate", "norm_final"]


def kernel(**inputs):
    import numpy as _np
    import concourse.bacc as _bacc
    from concourse import mybir as _mybir
    from concourse.bass_utils import run_bass_kernel_spmd as _run

    nc = _bacc.Bacc("TRN2", target_bir_lowering=False, num_devices=1)
    arrays, args = {}, {}
    for name in _INS:
        a = _np.ascontiguousarray(inputs[name])
        arrays[f"in_{name}"] = a
        args[name] = nc.dram_tensor(f"in_{name}", a.shape, _mybir.dt.from_np(a.dtype), kind="ExternalInput").ap()
    shape = arrays["in_x"].shape
    out = nc.dram_tensor("out_0", shape, _mybir.dt.float32, kind="ExternalOutput").ap()
    trunk(nc, args, out)
    r = _run(nc, [arrays], core_ids=[0])
    return r.results[0]["out_0"]
```

```python
from contextlib import ExitStack

import concourse.bass as bass
from concourse import mybir

F32 = mybir.dt.float32
F32R = mybir.dt.float32r
ALU = mybir.AluOpType
ACT = mybir.ActivationFunctionType
AX = mybir.AxisListType

P = 128
EPS = 1e-6
NB = 512
KC = 16
HALVES = 8
TILES = 4
BLOCKS = 4
SLOTS = 4


FIELDS = ("b", "a", "T", "t", "xh", "s", "sg")


class Place:

    def __init__(self, n):
        self.b, self.a, self.T, self.t, self.xh, self.s, self.sg = (n[f] for f in FIELDS)

    def counts(self):
        return dict(zip(FIELDS, (self.b, self.a, self.T, self.t, self.xh, self.s, self.sg)))


class Unit(Place):

    def __init__(self, kind, at, per):
        super().__init__(at)
        self.kind, self.per = kind, dict(per)

    def shifted(self, by, rounds):
        n = self.counts()
        return Unit(self.kind, {f: n[f] + rounds * by[f] if by[f] else n[f] for f in FIELDS}, self.per)


class Result(Place):

    def __init__(self, unit, j):
        n, per = unit.counts(), unit.per
        super().__init__({f: n[f] + per[f] * j if f in per else n[f] for f in FIELDS})
        self.kind, self.j, self.pair = unit.kind, j, j % 2
        self.transposed = "T" in per


class Steps:

    def __init__(self, engine, sem):
        self.engine, self.sem, self.n, self.emitted = engine, sem, 0, 0

    def mark(self, instruction):
        instruction.then_inc(self.sem, 1)
        self.n = self.n + 1
        self.emitted += 1
        return self.n

    def wait(self, n=None):
        self.engine.wait_ge(self.sem, self.n if n is None else n)

    def loop(self, i, start, per):
        self.kept = (self.n, self.emitted, start, per)
        if per:
            self.n = self.n + (i - start) * per

    def end(self, stop):
        n, emitted, start, per = self.kept
        assert self.emitted - emitted == per, (self.emitted - emitted, per)
        self.n = n + (stop - start) * per


def trunk(nc, t_in, out):
    x, p = t_in["x"], t_in["p"]
    _, SEQ, D = x.shape
    DEPTH, _, _, PLE = p.shape
    WA = t_in["cf_w_dw"].shape[1]
    WB = t_in["sc_w_conv"].shape[1]
    assert SEQ == 2 * P and D == KC * P == BLOCKS * NB and DEPTH == 2 and PLE == 2 * P
    GROUPS = t_in["mlp_w1"].shape[2] // D
    PAD = WA - 1
    SHARES = 2 * HALVES
    POOL_TAPS = 20

    def share(i):
        return WA * i // SHARES

    ROW_DW, ROW_BDW, ROW_CFN = 0, WA, WA + 1
    ROW_MIX, ROW_MLP, ROW_PLE, ROW_SC = WA + 2, WA + 4, WA + 6, WA + 8
    NROWS = ROW_SC + WB
    ROW_LOADS = 8

    at = dict(b=0, a=0, T=BLOCKS, t=0, xh=BLOCKS, s=BLOCKS, sg=0)

    def place(kind, per, blocks=BLOCKS):
        u = Unit(kind, at, dict(per, b=1, a=1))
        for f in FIELDS:
            n = u.per.get(f, 0)
            at[f] += n * BLOCKS if f not in "ba" else blocks
        return u

    pw1 = Unit("glu", dict(at, b=1, a=1), dict(b=2, a=2, T=1, t=1, sg=1))
    EMB_B, EMB_T = 2 * BLOCKS, 2 * BLOCKS - 1
    LAST_GLU_T = EMB_T + 1
    at.update(b=EMB_B + 1, a=EMB_B + HALVES, T=LAST_GLU_T + 1, t=BLOCKS,
              xh=2 * BLOCKS + 1, sg=2 * BLOCKS)
    RES = dict(T=1, t=1, xh=1, s=1)
    pw2 = place("pw2", RES)
    HID = dict(T=1, t=1, xh=1)

    def place_mlp():
        up, down = [], []
        up.append(place("hidden", HID))
        for g in range(GROUPS):
            down_after = g < GROUPS - 1
            down.append(place("add" if down_after else "mlp_out", {} if down_after else RES))
            if down_after:
                up.append(place("hidden", HID))
        return up, down

    mlp = [place_mlp()]
    gate = [place("gate", dict(RES, sg=1))]
    win = Unit("win", at, dict(b=3, a=3, T=2, t=2, xh=1))
    for f, n in dict(b=3, a=3, T=2, t=2, xh=1).items():
        at[f] += n * BLOCKS
    wout = place("w_out", RES)
    mlp.append(place_mlp())
    gate.append(place("gate_last", dict(t=1, s=1, sg=1)))

    NORM_CONV, NORM_MLP, NORM_PLE, NORM_WIN, NORM_FINAL = 1, (2, 5), (3, 6), 4, 7

    def distance(u, v):
        return {f: v.counts()[f] - u.counts()[f] for f in FIELDS}

    ctx = ExitStack()
    with ctx:
        def sb(name, shape, dt=F32):
            return ctx.enter_context(nc.sbuf_tensor(name, shape, dt))

        def sem(name):
            return ctx.enter_context(nc.semaphore(name))

        h = sb("h", [P, 2, D])
        conv = h[:, :, :].rearrange("p m (c n) -> p (m c) n", n=2 * P)
        X = [(sb("a_hi", [P, KC, 2 * P], F32R), sb("a_lo", [P, KC, 2 * P], F32R)),
             (sb("b_hi", [P, KC, 2 * P], F32R), sb("b_lo", [P, KC, 2 * P], F32R))]
        raw = sb("raw", [P, TILES, 4, NB])
        whi = sb("whi", [P, SLOTS, 2, NB], F32R)
        wlo = sb("wlo", [P, SLOTS, 2, NB], F32R)
        emb = sb("emb", [P, DEPTH, 2, D])
        rows = emb[0:NROWS, 0, 0, :]
        vpad = sb("vpad", [P, 4, PAD + 2 * P])
        res = sb("res", [P, 2, NB])
        work = sb("work", [P, 4, NB])
        zb = work[:, 0:2, :]
        val = work[:, 2:4, :]
        bias2 = work[:, :, :].rearrange("p c n -> p (c n)")
        prows = sb("prows", [P, DEPTH, 2, PLE])
        bias = sb("bias", [P, 2, NB])
        prod = sb("prod", [P, 2, 2, 2 * P])
        junk = prod[:, 0, :, :].rearrange("p c n -> p (c n)")
        vec = sb("vec", [P, KC, NROWS])
        ident = sb("ident", [P, P])
        ss = sb("ss", [P, 2, BLOCKS])
        rinv = sb("rinv", [P, 2])
        mean = sb("mean", [P, 2])
        root = sb("root", [P, 2])
        ones = bias[:, 0, 0:P]
        rb = bias[:, 1, 0:2 * P]
        y3 = zb.rearrange("p m (c n) -> p (m c) n", n=2 * P)
        tmps = [y3, val.rearrange("p m (c n) -> p (m c) n", n=2 * P)]
        rb_parts = res[:, 0, 0:2 * P], res[:, 1, 0:2 * P]

        acc = ctx.enter_context(nc.psum_tensor("acc", [P, 6, NB], F32))
        tp = ctx.enter_context(nc.psum_tensor("tp", [P, 4, 2 * P], F32))

        def x_banks(j):
            return tp if j == BLOCKS - 1 else acc[:, 2 * j:2 * j + 2, :].rearrange("p a (c n) -> p (a c) n", n=2 * P)

        ssb = acc[:, 4, 0:2 * P]

        raw_ready = [sem(f"raw_ready{q}") for q in range(TILES)]
        emb_ready = [sem(f"emb_ready{q}") for q in range(TILES)]
        hi_ready, lo_ready, half_used = sem("hi_ready"), sem("lo_ready"), sem("half_used")
        acc_free = sem("acc_free")
        res_ready = sem("res_ready")
        tp_done, tp_free = sem("tp_done"), sem("tp_free")
        xhi_ready, y_ready = sem("xhi_ready"), sem("y_ready")
        ss_ready, junk_written = sem("ss_ready"), sem("junk_written")
        sig_ready = sem("sig_ready")
        vpad_ready, conv_dve = sem("vpad_ready"), sem("conv_dve")
        prod_ready, prod_used, ones_ready = sem("prod_ready"), sem("prod_used"), sem("ones_ready")
        n_ready, y_full, y3_ready = sem("n_ready"), sem("y_full"), sem("y3_ready")
        mean_ready, root_ready = sem("mean_ready"), sem("root_ready")
        sq_ready, sq_used = sem("sq_ready"), sem("sq_used")
        const_ready, rows_ready, p_ready, vec_ready = (
            sem("const_ready"), sem("rows_ready"), sem("p_ready"), sem("vec_ready"))
        x_ready = [sem(f"x_ready{j}") for j in range(BLOCKS)]
        bias_ready, bias2_ready = sem("bias_ready"), sem("bias2_ready")
        reload_ready, final_ready, final_done, out_done = (
            sem("reload_ready"), sem("final_ready"), sem("final_done"), sem("out_done"))
        dve_step = sem("dve_step")

        block = ctx.enter_context(nc.Block())

        def summed(j):
            return (WA - 1) * j + (POOL_TAPS if j == BLOCKS - 1 else WA) - 1 + 2

        def cols(j):
            return bass.ds(j * NB, NB)

        def xtok(j):
            return x[0, :, j * NB:(j + 1) * NB].rearrange("(m q) n -> q m n", q=P)

        @block.sync
        def _(sp):
            def tile(b, q, src):
                if not (isinstance(b, int) and b == 0):
                    sp.wait_ge(lo_ready, HALVES * b - HALVES + 2 * q + 2)
                nc.sync.dma_start(raw[:, q, :, :], src).then_inc(raw_ready[q], 16)

            def load(b, w, col, row=0):
                for q in range(TILES):
                    tile(b, q, w[bass.ds(row + q * 4 * P, 4 * P), bass.ds(col, NB)]
                         .rearrange("(c r) n -> r c n", r=P))

            def load_unit(unit, w, col=0, row=0):
                with sp.Fori(0, BLOCKS) as j:
                    load(unit.b + j, w, j * NB + col, row)

            def load_mlp(layer):
                up, down = mlp[layer]
                w1, w2 = t_in["mlp_w1"][layer], t_in["mlp_w2"][layer]
                by = distance(up[0], up[1])
                with sp.Fori(0, GROUPS) as g:
                    load_unit(up[0].shifted(by, g), w1, col=g * D)
                    load_unit(down[0].shifted(by, g), w2, row=g * D)

            for j in range(BLOCKS):
                nc.sync.dma_start(h[:, :, j * NB:(j + 1) * NB], xtok(j)).then_inc(x_ready[j], 16)
                if j == 0:
                    w = t_in["cf_w_pw1"][0]
                    load(0, w, 0)
            load(1, w, D)
            with sp.Fori(1, BLOCKS) as j:
                load(2 * j, w, j * NB)
                load(2 * j + 1, w, j * NB + D)
            for q in range(TILES):
                w, n0 = t_in["ple_w_proj"][q // 2], (q % 2) * 2 * NB
                sp.wait_ge(lo_ready, HALVES * EMB_B - HALVES + 2 * q + 2)
                for s, ready in enumerate((raw_ready[q], emb_ready[q])):
                    nc.sync.dma_start(raw[:, q, 2 * s:2 * s + 2, :], w[:, n0 + s * NB:n0 + (s + 1) * NB]
                                      .rearrange("(c r) n -> r c n", r=P)).then_inc(ready, 16)
            load_unit(pw2, t_in["cf_w_pw2"][0])
            load_mlp(0)
            load_unit(gate[0], t_in["ple_w_gate"][0])
            with sp.Fori(1, BLOCKS + 1) as j:
                for part, first in ((0, D), (1, 2 * D), (2, 0)):
                    load(win.b - 3 + 3 * j + part, t_in["sc_w_in"][0], j * NB + first - NB)
            load_unit(wout, t_in["sc_w_out"][0])
            load_mlp(1)
            load_unit(gate[1], t_in["ple_w_gate"][1])
            sp.wait_ge(lo_ready, HALVES * at["b"])
            nc.sync.dma_start(raw[:, 2, :, :].rearrange("p c n -> p (c n)"),
                              t_in["norm_final"].partition_broadcast(P)).then_inc(final_ready, 16)
            for m in range(2):
                for part in range(2):
                    sp.wait_ge(final_done, 2 * m + part + 1)
                    nc.sync.dma_start(out[0, m * P:(m + 1) * P, part * D // 2:(part + 1) * D // 2],
                                      raw[:, m, 2 * part:2 * part + 2, :].rearrange("p c n -> p (c n)")
                                      ).then_inc(out_done, 16)
            sp.wait_ge(out_done, 64)

        @block.tensor
        def _(pe):
            def transpose_group(parts, dst=tp):
                for c, m, src in parts:
                    last = nc.tensor.transpose(dst[:, c, m * P:(m + 1) * P], src, ident[:, :])
                last.then_inc(tp_done, 1)

            def half(b, e, pair, xhi, xlo, chunks, first, last):
                pe.wait_ge(lo_ready, HALVES * b + e + 1)
                for m in range(2):
                    o = acc[:, bass.ds(2 * pair + m, 1), :]
                    s = slice(m * P, (m + 1) * P)
                    for c, k in enumerate(chunks):
                        hi, lo = whi[:, e % SLOTS, c, :], wlo[:, e % SLOTS, c, :]
                        nc.tensor.matmul(o, xhi[:, k, s], hi, start=first and c == 0, stop=False)
                        nc.tensor.matmul(o, xhi[:, k, s], lo, start=False, stop=False)
                        mm = nc.tensor.matmul(o, xlo[:, k, s], hi, start=False, stop=last and c == 1)
                mm.then_inc(half_used, 1)

            def multiply(b, a, pair, xin, pre=None, ready=None, behind=3):
                xhi, xlo = xin
                if not (isinstance(a, int) and a < 2):
                    pe.wait_ge(acc_free, a - 1)
                for e in range(HALVES):
                    if ready and e % 2 == 0:
                        pe.wait_ge(ready[0], ready[1] + e // 2 + 1)
                    half(b, e, pair, xhi, xlo, (2 * e, 2 * e + 1), e == 0, e == HALVES - 1)
                    if e == behind and pre is not None:
                        pe.wait_ge(res_ready, pre[1] + 1)
                        pe.wait_ge(tp_free, pre[0])
                        transpose_group((c, m, res[:, m, c * P:(c + 1) * P])
                                        for c in range(4) for m in range(2))

            def multiply_unit(unit, xin, ready, before=None):
                pre = (before.T, before.t) if before is not None and before.transposed else None
                multiply(unit.b, unit.a, 0, xin, pre, ready)
                with pe.Fori(1, BLOCKS) as j:
                    r = Result(unit, j - 1)
                    multiply(unit.b + j, unit.a + j, j % 2, xin,
                             (r.T, r.t) if r.transposed else None)

            def multiply_mlp(layer, u, ready, before):
                up, down = mlp[layer]
                hid = 1 - u
                by = distance(up[0], up[1])
                multiply_unit(up[0], X[u], ready, before)
                with pe.Fori(0, GROUPS - 1) as g:
                    w2, w1 = down[0].shifted(by, g), up[1].shifted(by, g)
                    multiply_unit(w2, X[hid], (tp_free, up[0].shifted(by, g).T),
                                  Result(up[0].shifted(by, g), BLOCKS - 1))
                    multiply_unit(w1, X[u], None, Result(w2, BLOCKS - 1))
                multiply_unit(down[-1], X[hid], (tp_free, up[-1].T), Result(up[-1], BLOCKS - 1))

            pe.wait_ge(const_ready, 3)
            pe.wait_ge(rows_ready, 16 * ROW_LOADS)
            for c in range(KC):
                v = tp[:, 2 * (c // 8):2 * (c // 8) + 2, :].rearrange("p c n -> p (c n)")
                last = nc.tensor.transpose(v[:, (c % 8) * NROWS:(c % 8 + 1) * NROWS],
                                           rows[:, c * P:(c + 1) * P], ident[0:NROWS, 0:NROWS])
            last.then_inc(vec_ready, 1)
            for j in range(BLOCKS):
                pe.wait_ge(x_ready[j], 16)
                if j == BLOCKS - 1:
                    pe.wait_ge(vec_ready, 2)
                transpose_group(((c, m, h[:, m, (4 * j + c) * P:(4 * j + c + 1) * P])
                                 for c in range(4) for m in range(2)), x_banks(j))

            multiply(0, 0, 0, X[0], None, (tp_free, 0))
            multiply(1, 1, 1, X[0])
            with pe.Fori(1, BLOCKS) as j:
                r = Result(pw1, j - 1)
                multiply(2 * j, 2 * j, 0, X[0], (r.T, r.t), behind=1)
                multiply(2 * j + 1, 2 * j + 1, 1, X[0])

            pe.wait_ge(p_ready, 16 * DEPTH)
            pe.wait_ge(tp_free, EMB_T)
            transpose_group((2 * l + c, m, prows[:, l, m, c * P:(c + 1) * P])
                            for l in range(DEPTH) for c in range(2) for m in range(2))
            pe.wait_ge(tp_free, EMB_T + 1)
            for e in range(HALVES):
                pe.wait_ge(acc_free, EMB_B + e - 1)
                l = e // BLOCKS
                half(EMB_B, e, e % 2, X[0][0], X[0][1], (2 * l, 2 * l + 1), True, True)
                if e == 1:
                    pe.wait_ge(res_ready, BLOCKS)
                    transpose_group((c, m, res[:, m, c * P:(c + 1) * P])
                                    for c in range(4) for m in range(2))
            pe.wait_ge(ones_ready, 1)
            for j in range(BLOCKS):
                pe.wait_ge(sq_ready, j + 1)
                for c in range(4):
                    mm = nc.tensor.matmul(ssb, ones, tmps[j % 2][:, c, :],
                                          start=j == 0 and c == 0, stop=j == BLOCKS - 1 and c == 3)
                mm.then_inc(sq_used, 1)

            multiply_unit(pw2, X[1], (y_ready, 0))
            multiply_mlp(0, 0, (tp_free, pw2.T), Result(pw2, BLOCKS - 1))
            multiply_unit(gate[0], X[0], (tp_free, mlp[0][1][-1].T), Result(mlp[0][1][-1], BLOCKS - 1))

            r = Result(gate[0], BLOCKS - 1)
            multiply(win.b, win.a, 0, X[1], (r.T, r.t), (tp_free, gate[0].T))
            multiply(win.b + 1, win.a + 1, 1, X[1])
            multiply(win.b + 2, win.a + 2, 2, X[1], (win.T, win.t))
            with pe.Fori(1, BLOCKS) as j:
                multiply(win.b + 3 * j, win.a + 3 * j, 0, X[1], (win.T + 2 * j - 1, win.t + 2 * j - 1))
                multiply(win.b + 3 * j + 1, win.a + 3 * j + 1, 1, X[1])
                multiply(win.b + 3 * j + 2, win.a + 3 * j + 2, 2, X[1], (win.T + 2 * j, win.t + 2 * j))
            multiply(wout.b, wout.a, 0, X[0], (wout.T - 1, wout.t - 1), (y_ready, BLOCKS))
            with pe.Fori(1, BLOCKS) as j:
                r = Result(wout, j - 1)
                multiply(wout.b + j, wout.a + j, j % 2, X[0], (r.T, r.t))
            multiply_mlp(1, 1, (tp_free, wout.T), Result(wout, BLOCKS - 1))
            multiply_unit(gate[1], X[1], (tp_free, mlp[1][1][-1].T), Result(mlp[1][1][-1], BLOCKS - 1))

        @block.scalar
        def _(act):
            def split_hi(b, e):
                if e % 2 == 0:
                    act.wait_ge(raw_ready[e // 2], 16 * b + 16)
                elif isinstance(b, int) and b == EMB_B:
                    act.wait_ge(emb_ready[e // 2], 16)
                if not (isinstance(b, int) and b == 0 and e < SLOTS):
                    act.wait_ge(half_used, HALVES * b + e + 1 - SLOTS)
                nc.scalar.activation(whi[:, e % SLOTS, :, :],
                                     raw[:, e // 2, 2 * (e % 2):2 * (e % 2) + 2, :],
                                     ACT.Copy).then_inc(hi_ready, 1)

            def squares(n, src, j):
                for m in range(2):
                    if m:
                        act.wait_ge(junk_written, n + 1)
                    elif not (isinstance(n, int) and n == 0):
                        act.wait_ge(ss_ready, n)
                    ins = nc.scalar.activation(junk, src(m), ACT.Square,
                                               accum_out=ss[:, m, bass.ds(j, 1)])
                    ins.then_inc(ss_ready if m else junk_written, 1)

            def process(r):
                if r.kind == "hidden":
                    act.wait_ge(acc_free, r.a + 1)
                    act.wait_ge(tp_done, r.T)
                    nc.scalar.activation(res[:, :, :], zb, ACT.Square).then_inc(res_ready, 1)
                if r.kind in ("glu", "gate", "gate_last"):
                    act.wait_ge(acc_free, r.a + 1)
                    nc.scalar.activation(zb, zb, ACT.Sigmoid).then_inc(sig_ready, 1)
                if r.kind in ("pw2", "mlp_out", "w_out"):
                    keep(r)

            def keep(r):
                act.wait_ge(res_ready, r.t + 1)
                nc.scalar.activation(h[:, :, cols(r.j)], res[:, :, :], ACT.Copy)
                squares(r.s, lambda m: res[:, m, :], r.j)

            def operand_hi(T, j, dst, gain=None, src=tp):
                act.wait_ge(tp_done, T + 1)
                if gain is None:
                    last = nc.scalar.activation(dst[0][:, bass.ds(4 * j, 4), :], src[:, :, :], ACT.Copy)
                else:
                    for c in range(4):
                        last = nc.scalar.activation(
                            dst[0][:, bass.ds(4 * j + c, 1), :], src[:, c:c + 1, :], ACT.Copy,
                            scale=vec[:, bass.ds(4 * j + c, 1), gain])
                last.then_inc(xhi_ready, 1)

            def to_vpad(T, n, products_made=WA * (BLOCKS - 1) + POOL_TAPS):
                act.wait_ge(tp_done, T + 1)
                act.wait_ge(conv_dve, n + 1)
                act.wait_ge(prod_ready, products_made + 1)
                nc.scalar.activation(vpad[:, :, PAD:], tp[:, :, :], ACT.Copy).then_inc(vpad_ready, 1)
                act.wait_ge(vpad_ready, n + 1)
                nc.scalar.sem_inc(tp_free, 1)

            def run(b, before=None, after=None, at=7, between=None):
                for e in range(HALVES):
                    if e == 3 and before:
                        before()
                    if e == at and after:
                        after()
                    split_hi(b, e)
                    if between:
                        between(e)

            def products(j, first, stop):
                for k in range(first, stop):
                    if k:
                        act.wait_ge(prod_used, (WA - 1) * j + k)
                    for c in range(2):
                        w = vec[:, bass.ds(4 * j + 2 + c, 1), ROW_DW + k]
                        src = vpad[:, 2 + c:3 + c, k:k + 2 * P]
                        if k == 0:
                            ins = nc.scalar.activation(conv[:, bass.ds(4 * j + 2 + c, 1), :], src, ACT.Identity,
                                                       scale=w, bias=vec[:, bass.ds(4 * j + 2 + c, 1), ROW_BDW])
                        else:
                            ins = nc.scalar.activation(prod[:, k % 2, c:c + 1, :], src, ACT.Copy, scale=w)
                    ins.then_inc(prod_ready, 1)

            def take_root(n, src=None, dst=None):
                act.wait_ge(mean_ready, n + 1)
                nc.scalar.activation(root[:, :] if dst is None else dst, mean[:, :] if src is None else src,
                                     ACT.Sqrt).then_inc(root_ready, 1)

            def run_behind(b, r, dst, gain=None, new_norm=None):
                def after():
                    if r.transposed:
                        operand_hi(r.T, r.j, dst, gain)
                    if new_norm is not None:
                        take_root(new_norm)

                def between(e):
                    if e == 4 and r.kind in ("gate", "gate_last"):
                        keep(r)
                run(b, lambda: process(r), after, between=between)

            def run_unit(u, dst, gain, prev, prev_dst, prev_gain, new_norm=None):
                run_behind(u.b, Result(prev, BLOCKS - 1), prev_dst, prev_gain, new_norm)
                with act.Fori(1, BLOCKS) as j:
                    run_behind(u.b + j, Result(u, j - 1), dst, gain)

            def run_mlp(layer, u, prev):
                up, down = mlp[layer]
                hid, gain = X[1 - u], ROW_PLE + layer
                by = distance(up[0], up[1])
                run_unit(up[0], hid, None, prev, X[u], ROW_MLP + layer, NORM_MLP[layer])
                with act.Fori(0, GROUPS - 1) as g:
                    w2, w1 = down[0].shifted(by, g), up[1].shifted(by, g)
                    run_unit(w2, None, None, up[0].shifted(by, g), hid, None)
                    run_unit(w1, hid, None, w2, None, None)
                run_unit(down[-1], X[u], gain, up[-1], hid, None)

            for r0, src in [(ROW_DW, t_in["cf_w_dw"][0, 0:16]), (ROW_DW + 16, t_in["cf_w_dw"][0, 16:WA]), (ROW_BDW, t_in["cf_b_dw"]),
                            (ROW_CFN, t_in["cf_norm"]), (ROW_MIX, t_in["norm_mix"]),
                            (ROW_MLP, t_in["norm_mlp"]), (ROW_PLE, t_in["norm_ple"]),
                            (ROW_SC, t_in["sc_w_conv"][0])]:
                nc.scalar.dma_start(rows[r0:r0 + src.shape[0], :], src).then_inc(rows_ready, 16)
            for l in range(DEPTH):
                nc.scalar.dma_start(prows[:, l, :, :],
                                    p[l, 0].rearrange("(m q) n -> q m n", q=P)).then_inc(p_ready, 16)
            act.wait_ge(vec_ready, 2)
            for j in range(BLOCKS):
                operand_hi(j, j, X[0], ROW_MIX, x_banks(j))
                if j < 2:
                    split_hi(0, 2 * j)
                    split_hi(0, 2 * j + 1)
            for j in range(BLOCKS):
                act.wait_ge(x_ready[j], 16)
                squares(j, lambda m: h[:, m, j * NB:(j + 1) * NB], j)
            for e in range(SLOTS, HALVES):
                split_hi(0, e)
                if e == HALVES - 1:
                    take_root(0)

            def some_products(j, i):
                products(j, share(i), share(i + 1))

            def pair(j, older):
                def between(e):
                    if e >= 6:
                        some_products(j - 1, e - 6)
                    elif older:
                        some_products(j - 2, 2 + HALVES + e)
                r = Result(pw1, j - 1)
                run(2 * j, lambda: process(r), lambda: to_vpad(r.T, r.j, WA * r.j), 6, between)
                run(2 * j + 1, None, None, 7, lambda e: some_products(j - 1, 2 + e))

            run(1)
            pair(1, False)
            with act.Fori(2, BLOCKS) as j:
                pair(j, True)

            def embedding_out(e):
                act.wait_ge(acc_free, EMB_B + e)
                act.wait_ge(half_used, HALVES * EMB_B + e + 1)
                nc.scalar.activation(emb[:, e // BLOCKS, :, (e % BLOCKS) * NB:(e % BLOCKS + 1) * NB],
                                     acc[:, 2 * (e % 2):2 * (e % 2) + 2, :],
                                     ACT.Copy).then_inc(acc_free, 1)

            for e in range(3):
                split_hi(EMB_B, e)
                some_products(BLOCKS - 2, 2 + HALVES + e)
            operand_hi(EMB_T, 0, X[0])
            behind_glu = share(2 + HALVES + 3) + 3
            products(BLOCKS - 2, share(2 + HALVES + 3), behind_glu)
            process(Result(pw1, BLOCKS - 1))
            split_hi(EMB_B, 3)
            products(BLOCKS - 2, behind_glu, WA)
            embedding_out(0)
            split_hi(EMB_B, 4)
            embedding_out(1)
            to_vpad(LAST_GLU_T, BLOCKS - 1, WA * (BLOCKS - 1))
            for e in range(5, HALVES + 3):
                if e < HALVES:
                    split_hi(EMB_B, e)
                embedding_out(e - 3)
                products(BLOCKS - 1, 4 * (e - 5), min(4 * (e - 4), POOL_TAPS))
            for j in range(BLOCKS):
                if j == BLOCKS - 1:
                    for e in range(SLOTS):
                        split_hi(pw2.b, e)
                act.wait_ge(conv_dve, j + 2)
                act.wait_ge(prod_used, summed(j))
                if j >= 2:
                    act.wait_ge(sq_used, j - 1)
                nc.scalar.activation(tmps[j % 2], conv[:, 4 * j:4 * j + 4, :],
                                     ACT.Square).then_inc(sq_ready, 1)

            def swish_sigmoid(j):
                act.wait_ge(n_ready, j + 1)
                act.wait_ge(sq_used, BLOCKS)
                if j >= 2:
                    act.wait_ge(y_full, j - 1)
                nc.scalar.activation(tmps[j % 2], conv[:, 4 * j:4 * j + 4, :],
                                     ACT.Sigmoid).then_inc(sig_ready, 1)

            def swish_hi(j):
                act.wait_ge(y_full, j + 1)
                nc.scalar.activation(X[1][0][:, 4 * j:4 * j + 4, :], conv[:, 4 * j:4 * j + 4, :],
                                     ACT.Copy).then_inc(xhi_ready, 1)

            take_root(NORM_CONV, *rb_parts)
            swish_sigmoid(0)
            for j in range(1, BLOCKS):
                swish_sigmoid(j)
                swish_hi(j - 1)
            swish_hi(BLOCKS - 1)
            for e in range(SLOTS, HALVES):
                split_hi(pw2.b, e)
            with act.Fori(1, BLOCKS) as j:
                run_behind(pw2.b + j, Result(pw2, j - 1), X[0], ROW_MLP)
            run_mlp(0, 0, pw2)
            run_unit(gate[0], X[1], ROW_MIX + 1, mlp[0][1][-1], X[0], ROW_PLE, NORM_PLE[0])

            def short_out_hi(j):
                act.wait_ge(y3_ready, j + 1)
                nc.scalar.activation(X[0][0][:, bass.ds(4 * j, 4), :], y3, ACT.Copy).then_inc(xhi_ready, 1)

            run_behind(win.b, Result(gate[0], BLOCKS - 1), X[1], ROW_MIX + 1, NORM_WIN)
            run(win.b + 1)
            run(win.b + 2, None, lambda: to_vpad(win.T, BLOCKS))
            with act.Fori(1, BLOCKS) as j:
                run(win.b + 3 * j, None, lambda: short_out_hi(j - 1))
                run(win.b + 3 * j + 1)
                run(win.b + 3 * j + 2, None, lambda: to_vpad(win.T + 2 * j, j + BLOCKS))
            run(wout.b, None, lambda: short_out_hi(BLOCKS - 1))
            with act.Fori(1, BLOCKS) as j:
                run_behind(wout.b + j, Result(wout, j - 1), X[1], ROW_MLP + 1)
            run_mlp(1, 1, wout)
            run_unit(gate[1], None, None, mlp[1][1][-1], X[1], ROW_PLE + 1, NORM_PLE[1])
            process(Result(gate[1], BLOCKS - 1))
            keep(Result(gate[1], BLOCKS - 1))
            take_root(NORM_FINAL)

        @block.vector
        def _(dve):
            steps = Steps(dve, dve_step)

            def split_lo(b, e):
                dve.wait_ge(hi_ready, HALVES * b + e + 1)
                nc.vector.tensor_tensor(wlo[:, e % SLOTS, :, :],
                                        raw[:, e // 2, 2 * (e % 2):2 * (e % 2) + 2, :],
                                        whi[:, e % SLOTS, :, :].bitcast(F32),
                                        ALU.subtract).then_inc(lo_ready, 1)

            def product(b, a):
                dve.wait_ge(half_used, HALVES * b + HALVES)
                if not (isinstance(a, int) and a == 0):
                    dve.wait_ge(acc_free, a)

            def pair_half(pair, m):
                return acc[:, bass.ds(2 * pair + m, 1), :]

            def scaled(dst, pair, bias_row=None):
                for m in range(2):
                    if bias_row is None:
                        last = nc.vector.tensor_scalar(dst[:, m:m + 1, :], pair_half(pair, m),
                                                       rinv[:, m:m + 1], None, ALU.mult)
                    else:
                        last = nc.vector.scalar_tensor_tensor(
                            dst[:, m:m + 1, :], pair_half(pair, m), rinv[:, m:m + 1],
                            bias[:, bias_row:bias_row + 1, :], ALU.mult, ALU.add)
                last.then_inc(acc_free, 1)

            def process(r):
                product(r.b, r.a)
                both = acc[:, bass.ds(2 * r.pair, 2), :]
                here = h[:, :, cols(r.j)]
                if r.kind == "hidden":
                    dve.wait_ge(res_ready, r.t)
                    for m in range(2):
                        last = nc.vector.tensor_scalar(zb[:, m:m + 1, :], pair_half(r.pair, m),
                                                       rinv[:, m:m + 1], 0.0, ALU.mult, ALU.max)
                    last.then_inc(acc_free, 1)
                    return
                if r.kind == "add":
                    dve.wait_ge(ss_ready, r.s)
                    nc.vector.tensor_tensor(here, both, here, ALU.add).then_inc(acc_free, 1)
                    return
                if r.kind in ("gate", "gate_last"):
                    scaled(zb, r.pair)
                    return
                dve.wait_ge(tp_done, r.T)
                dve.wait_ge(ss_ready, r.s)
                nc.vector.tensor_tensor(res[:, :, :], both, here, ALU.add).then_inc(acc_free, 1)
                dve.wait_ge(acc_free, r.a + 1)
                if r.kind == "pw2":
                    nc.vector.tensor_tensor(res[:, :, :], res[:, :, :],
                                            bias2[:, cols(r.j)].unsqueeze(1).to_broadcast([P, 2, NB]),
                                            ALU.add).then_inc(res_ready, 1)
                else:
                    nc.vector.sem_inc(res_ready, 1)

            def add_gated(r):
                dve.wait_ge(sig_ready, r.sg + 1)
                steps.mark(nc.vector.tensor_tensor(zb, zb, emb[:, 0 if r.kind == "gate" else 1, :, cols(r.j)],
                                                   ALU.mult))
                steps.wait()
                dve.wait_ge(tp_done, r.T)
                dve.wait_ge(ss_ready, r.s)
                nc.vector.tensor_tensor(res[:, :, :], zb, h[:, :, cols(r.j)], ALU.add).then_inc(res_ready, 1)

            def operand_lo(xh, j, dst, gain=None, src=tp):
                dve.wait_ge(xhi_ready, xh + 1)
                if gain is None:
                    last = nc.vector.tensor_tensor(dst[1][:, bass.ds(4 * j, 4), :], src[:, :, :],
                                                   dst[0][:, bass.ds(4 * j, 4), :].bitcast(F32),
                                                   ALU.subtract)
                else:
                    for c in range(4):
                        last = nc.vector.scalar_tensor_tensor(
                            dst[1][:, bass.ds(4 * j + c, 1), :], src[:, c:c + 1, :],
                            vec[:, bass.ds(4 * j + c, 1), gain],
                            dst[0][:, bass.ds(4 * j + c, 1), :].bitcast(F32), ALU.mult, ALU.subtract)
                last.then_inc(tp_free, 1)

            def inverse_root(n, total, m, y, t):
                nc.vector.tensor_scalar(m, total, 1.0 / D, EPS, ALU.mult, ALU.add).then_inc(mean_ready, 1)
                dve.wait_ge(root_ready, n + 1)
                steps.mark(nc.vector.reciprocal(y, t))
                steps.wait()
                steps.mark(nc.vector.tensor_tensor(t, y, y, ALU.mult))
                steps.wait()
                steps.mark(nc.vector.tensor_tensor(t, t, m, ALU.mult))
                steps.wait()
                steps.mark(nc.vector.tensor_scalar(t, t, -0.5, 1.5, ALU.mult, ALU.add))
                steps.wait()
                steps.mark(nc.vector.tensor_tensor(y, y, t, ALU.mult))
                steps.wait()

            def norm(n, groups):
                dve.wait_ge(ss_ready, groups)
                steps.mark(nc.vector.tensor_reduce(rinv[:, :], ss[:, :, :], AX.X, ALU.add))
                steps.wait()
                inverse_root(n, rinv[:, :], mean[:, :], rinv[:, :], root[:, :])

            def run(b, before=None, after=None, between=None):
                for e in range(HALVES):
                    if e == 3 and before:
                        before()
                    if e == 7 and after:
                        after()
                    split_lo(b, e)
                    if between:
                        between(e)

            def run_behind(b, r, dst, gain=None, new_norm=None):
                def after():
                    if r.transposed:
                        operand_lo(r.xh, r.j, dst, gain)
                    if new_norm is not None:
                        norm(*new_norm)

                def between(e):
                    if e == 3 and r.kind in ("gate", "gate_last"):
                        add_gated(r)
                run(b, lambda: process(r), after, between)

            def run_unit(u, dst, gain, prev, prev_dst, prev_gain, new_norm=None):
                run_behind(u.b, Result(prev, BLOCKS - 1), prev_dst, prev_gain,
                           None if new_norm is None else (new_norm, u.s))
                with dve.Fori(1, BLOCKS) as j:
                    steps.loop(j, 1, 1 if u.kind in ("gate", "gate_last") else 0)
                    run_behind(u.b + j, Result(u, j - 1), dst, gain)
                steps.end(BLOCKS)

            def run_mlp(layer, u, prev):
                up, down = mlp[layer]
                hid, gain = X[1 - u], ROW_PLE + layer
                by = distance(up[0], up[1])
                run_unit(up[0], hid, None, prev, X[u], ROW_MLP + layer, NORM_MLP[layer])
                with dve.Fori(0, GROUPS - 1) as g:
                    w2, w1 = down[0].shifted(by, g), up[1].shifted(by, g)
                    run_unit(w2, None, None, up[0].shifted(by, g), hid, None)
                    run_unit(w1, hid, None, w2, None, None)
                run_unit(down[-1], X[u], gain, up[-1], hid, None)

            nc.vector.sem_inc(conv_dve, 1)
            dve.wait_ge(vec_ready, 1)
            for bank in range(2):
                v = tp[:, 2 * bank:2 * bank + 2, :].rearrange("p c n -> p (c n)")
                last = nc.vector.tensor_copy(vec[:, 8 * bank:8 * bank + 8, :].rearrange("p c r -> p (c r)"),
                                             v[:, 0:8 * NROWS])
            last.then_inc(vec_ready, 1)
            for j in range(BLOCKS):
                operand_lo(j, j, X[0], ROW_MIX, x_banks(j))
                if j < 2:
                    split_lo(0, 2 * j)
                    split_lo(0, 2 * j + 1)
            for e in range(SLOTS, HALVES):
                split_lo(0, e)
            norm(0, BLOCKS)

            def value(j):
                product(2 * j, 2 * j)
                dve.wait_ge(bias_ready, 32 * j + 32)
                scaled(val, 0, 0)

            def glu(r):
                product(r.b, r.a)
                scaled(zb, 1, 1)
                dve.wait_ge(sig_ready, r.sg + 1)
                dve.wait_ge(tp_done, r.T)
                nc.vector.tensor_tensor(res[:, :, :], val, zb, ALU.mult).then_inc(res_ready, 1)

            def taps(j, first, stop, chunks=(0, 1)):
                for k in range(first, stop):
                    for c in chunks:
                        if k:
                            steps.wait(steps.n - 1)
                        o = conv[:, bass.ds(4 * j + c, 1), :]
                        w = vec[:, bass.ds(4 * j + c, 1), ROW_DW + k]
                        src = vpad[:, c:c + 1, k:k + 2 * P]
                        if k == 0:
                            ins = nc.vector.tensor_scalar(o, src, w, vec[:, bass.ds(4 * j + c, 1), ROW_BDW],
                                                          ALU.mult, ALU.add)
                        else:
                            ins = nc.vector.scalar_tensor_tensor(o, src, w, o, ALU.mult, ALU.add)
                        if k == WA - 1 and c == (3 if isinstance(j, int) and j == BLOCKS - 1 else 1):
                            ins.then_inc(conv_dve, 1)
                        else:
                            steps.mark(ins)

            def some_taps(j, i):
                if i == 0:
                    dve.wait_ge(vpad_ready, j + 1)
                taps(j, share(i), share(i + 1))

            def pair(j, older):
                def between(e):
                    if e >= 5:
                        some_taps(j - 1, e - 5)
                    elif older:
                        some_taps(j - 2, 3 + HALVES + e)
                r = Result(pw1, j - 1)
                run(2 * j, lambda: glu(r), None, between)
                run(2 * j + 1, lambda: value(j), None, lambda e: some_taps(j - 1, 3 + e))

            run(1, lambda: value(0))
            pair(1, False)
            with dve.Fori(2, BLOCKS) as j:
                steps.loop(j, 2, 2 * WA - 1)
                pair(j, True)
            steps.end(BLOCKS)

            r = Result(pw1, BLOCKS - 1)
            for e in range(3):
                split_lo(EMB_B, e)
                if e == 2:
                    operand_lo(BLOCKS, 0, X[0])
                some_taps(BLOCKS - 2, 3 + HALVES + e)
            glu(r)
            split_lo(EMB_B, 3)
            taps(BLOCKS - 2, share(3 + HALVES + 3), WA)
            split_lo(EMB_B, 4)
            dve.wait_ge(vpad_ready, BLOCKS)
            for e in range(5, HALVES):
                taps(BLOCKS - 1, 5 * (e - 5), 5 * (e - 4))
                split_lo(EMB_B, e)
            taps(BLOCKS - 1, 5 * (HALVES - 5), WA)
            dve.wait_ge(prod_used, summed(BLOCKS - 1))
            taps(BLOCKS - 1, POOL_TAPS, WA, (2, 3))
            for e in range(SLOTS):
                split_lo(pw2.b, e)
            dve.wait_ge(sq_used, BLOCKS)
            inverse_root(NORM_CONV, ssb, rb_parts[0], rb, rb_parts[1])

            def normalise(j):
                dve.wait_ge(prod_used, summed(j))
                dve.wait_ge(conv_dve, j + 2)
                for c in range(4 * j, 4 * j + 4):
                    last = nc.vector.scalar_tensor_tensor(conv[:, c, :], conv[:, c, :],
                                                          vec[:, c, ROW_CFN:ROW_CFN + 1], rb,
                                                          ALU.mult, ALU.mult)
                last.then_inc(n_ready, 1)

            def swish(j):
                dve.wait_ge(sig_ready, BLOCKS + j + 1)
                g = conv[:, 4 * j:4 * j + 4, :]
                nc.vector.tensor_tensor(g, g, tmps[j % 2], ALU.mult).then_inc(y_full, 1)

            def swish_lo(j):
                dve.wait_ge(xhi_ready, BLOCKS + 1 + j + 1)
                dve.wait_ge(y_full, j + 1)
                nc.vector.tensor_tensor(X[1][1][:, 4 * j:4 * j + 4, :], conv[:, 4 * j:4 * j + 4, :],
                                        X[1][0][:, 4 * j:4 * j + 4, :].bitcast(F32),
                                        ALU.subtract).then_inc(y_ready, 1)

            normalise(0)
            for j in range(BLOCKS):
                if j + 1 < BLOCKS:
                    normalise(j + 1)
                swish(j)
                if j:
                    swish_lo(j - 1)
            swish_lo(BLOCKS - 1)
            for e in range(SLOTS, HALVES):
                split_lo(pw2.b, e)
            dve.wait_ge(reload_ready, 32)
            dve.wait_ge(bias2_ready, 16)
            with dve.Fori(1, BLOCKS) as j:
                run_behind(pw2.b + j, Result(pw2, j - 1), X[0], ROW_MLP)
            run_mlp(0, 0, pw2)
            run_unit(gate[0], X[1], ROW_MIX + 1, mlp[0][1][-1], X[0], ROW_PLE, NORM_PLE[0])

            def gate_c(a):
                product(a[0], a[1])
                scaled(val, 0)

            def c_times_v(j):
                product(win.b + 3 * j + 1, win.a + 3 * j + 1)
                dve.wait_ge(tp_done, win.T + 2 * j)
                for m in range(2):
                    last = nc.vector.scalar_tensor_tensor(res[:, m:m + 1, :], pair_half(1, m), rinv[:, m:m + 1],
                                                          val[:, m:m + 1, :], ALU.mult, ALU.mult)
                last.then_inc(acc_free, 1)
                dve.wait_ge(acc_free, win.a + 3 * j + 2)
                nc.vector.sem_inc(res_ready, 1)

            def gate_b(j):
                product(win.b + 3 * j + 2, win.a + 3 * j + 2)
                dve.wait_ge(tp_done, win.T + 2 * j + 1)
                scaled(res, 2)
                dve.wait_ge(acc_free, win.a + 3 * j + 3)
                nc.vector.sem_inc(res_ready, 1)

            def short_taps(j):
                dve.wait_ge(vpad_ready, j + BLOCKS + 1)
                for k in range(WB):
                    if k:
                        steps.wait()
                    for c in range(4):
                        w = vec[:, bass.ds(4 * j + c, 1), ROW_SC + k]
                        src = vpad[:, c:c + 1, PAD - WB + 1 + k:PAD - WB + 1 + k + 2 * P]
                        o = y3[:, c:c + 1, :]
                        if k == 0:
                            ins = nc.vector.tensor_scalar(o, src, w, None, ALU.mult)
                        else:
                            ins = nc.vector.scalar_tensor_tensor(o, src, w, o, ALU.mult, ALU.add)
                        if k == WB - 1 and c == 3:
                            ins.then_inc(conv_dve, 1)
                        else:
                            steps.mark(ins)

            def short_out(j):
                dve.wait_ge(tp_done, win.T + 2 * j + 2)
                dve.wait_ge(conv_dve, j + BLOCKS + 2)
                steps.mark(nc.vector.tensor_tensor(y3, tp[:, :, :], y3, ALU.mult))
                steps.wait()
                nc.vector.sem_inc(tp_free, 1)
                nc.vector.sem_inc(y3_ready, 1)
                dve.wait_ge(xhi_ready, win.xh + j + 1)
                nc.vector.tensor_tensor(X[0][1][:, bass.ds(4 * j, 4), :], y3,
                                        X[0][0][:, bass.ds(4 * j, 4), :].bitcast(F32),
                                        ALU.subtract).then_inc(y_ready, 1)

            run_behind(win.b, Result(gate[0], BLOCKS - 1), X[1], ROW_MIX + 1, (NORM_WIN, win.s))
            run(win.b + 1, lambda: gate_c((win.b, win.a)))
            run(win.b + 2, lambda: c_times_v(0), None, lambda e: short_taps(0) if e == 7 else None)
            with dve.Fori(1, BLOCKS) as j:
                steps.loop(j, 1, 4 * WB)
                run(win.b + 3 * j, lambda: gate_b(j - 1), lambda: short_out(j - 1))
                run(win.b + 3 * j + 1, lambda: gate_c((win.b + 3 * j, win.a + 3 * j)))
                run(win.b + 3 * j + 2, lambda: c_times_v(j), None,
                    lambda e: short_taps(j) if e == 7 else None)
            steps.end(BLOCKS)
            run(wout.b, lambda: gate_b(BLOCKS - 1), lambda: short_out(BLOCKS - 1))
            with dve.Fori(1, BLOCKS) as j:
                run_behind(wout.b + j, Result(wout, j - 1), X[1], ROW_MLP + 1)
            run_mlp(1, 1, wout)
            run_unit(gate[1], None, None, mlp[1][1][-1], X[1], ROW_PLE + 1, NORM_PLE[1])
            process(Result(gate[1], BLOCKS - 1))
            add_gated(Result(gate[1], BLOCKS - 1))
            norm(NORM_FINAL, at["s"])
            dve.wait_ge(final_ready, 16)
            flat = raw[:, :, :, :].rearrange("p q c n -> p q (c n)")
            for m in range(2):
                for part in range(2):
                    half = slice(part * D // 2, (part + 1) * D // 2)
                    nc.vector.scalar_tensor_tensor(flat[:, m, half], h[:, m, half], rinv[:, m:m + 1],
                                                   flat[:, 2, half], ALU.mult, ALU.mult).then_inc(final_done, 1)

        @block.gpsimd
        def _(pool):
            nc.gpsimd.sem_inc(prod_ready, 1)
            nc.gpsimd.sem_inc(prod_used, 2)
            nc.gpsimd.memset(ident[:, :], 0.0).then_inc(const_ready, 1)
            nc.gpsimd.memset(vpad[:, :, 0:PAD], 0.0).then_inc(const_ready, 1)
            pool.wait_ge(const_ready, 2)
            nc.gpsimd.affine_select(out=ident[:, :], in_=ident[:, :], compare_op=ALU.not_equal, fill=1.0,
                                    base=0, pattern=[[-1, P]], channel_multiplier=1).then_inc(const_ready, 1)

            def load_bias(j):
                for half in range(2):
                    nc.gpsimd.dma_start(bias[:, half, :], t_in["cf_b_pw1"][0, bass.ds(j * NB + half * D, NB)]
                                        .partition_broadcast(P)).then_inc(bias_ready, 16)

            def add_up(j):
                o = conv[:, 4 * j + 2:4 * j + 4, :]
                for k in range(1, POOL_TAPS if j == BLOCKS - 1 else WA):
                    pool.wait_ge(prod_ready, WA * j + k + 2)
                    pool.wait_ge(prod_used, (WA - 1) * j + k - 1 + 2)
                    nc.gpsimd.tensor_tensor(o, prod[:, k % 2, :, :], o, ALU.add).then_inc(prod_used, 1)

            load_bias(0)
            for j in range(1, BLOCKS):
                pool.wait_ge(acc_free, 2 * j)
                load_bias(j)
                add_up(j - 1)
            pool.wait_ge(acc_free, 2 * BLOCKS)
            nc.gpsimd.memset(ones, 1.0).then_inc(ones_ready, 1)
            add_up(BLOCKS - 1)
            for m in range(2):
                pool.wait_ge(y_ready, 2 * m + 2)
                nc.gpsimd.dma_start(h[:, m, :], x[0, m * P:(m + 1) * P, :]).then_inc(reload_ready, 16)
            nc.gpsimd.dma_start(bias2, t_in["cf_b_pw2"][0].partition_broadcast(P)).then_inc(bias2_ready, 16)


_INS = ["x", "p", "norm_mix", "norm_mlp", "norm_ple", "cf_w_pw1", "cf_b_pw1", "cf_w_dw", "cf_b_dw",
        "cf_norm", "cf_w_pw2", "cf_b_pw2", "sc_w_in", "sc_w_conv", "sc_w_out", "mlp_w1", "mlp_w2",
        "ple_w_proj", "ple_w_gate", "norm_final"]


def kernel(**inputs):
    import numpy as _np
    import concourse.bacc as _bacc
    from concourse import mybir as _mybir
    from concourse.bass_utils import run_bass_kernel_spmd as _run

    nc = _bacc.Bacc("TRN2", target_bir_lowering=False, num_devices=1)
    arrays, args = {}, {}
    for name in _INS:
        a = _np.ascontiguousarray(inputs[name])
        arrays[f"in_{name}"] = a
        args[name] = nc.dram_tensor(f"in_{name}", a.shape, _mybir.dt.from_np(a.dtype), kind="ExternalInput").ap()
    shape = arrays["in_x"].shape
    out = nc.dram_tensor("out_0", shape, _mybir.dt.float32, kind="ExternalOutput").ap()
    trunk(nc, args, out)
    r = _run(nc, [arrays], core_ids=[0])
    return r.results[0]["out_0"]
```
